# Optimizing a Trainium2 kernel written in Bass

```python
import math
import jax, jax.numpy as jnp
from jax import lax
import numpy as np

D_MODEL = 1024
BATCH = 1
SEQ = 512
DEPTH = 2

N_HEADS_A = 4
DIFF_QK_DIM = 64
DIFF_V_DIM = 128
N_HEADS_B = 4
SB_DIM = 64
N_GROUPS_C = 4
SGU_DIM = 64
CHUNK = 128
QBLOCK = 128
WIDTH_A = N_HEADS_A * DIFF_V_DIM
WIDTH_B = N_HEADS_B * SB_DIM
WIDTH_C = N_GROUPS_C * SGU_DIM
D_MIX = WIDTH_A + WIDTH_B + WIDTH_C
IN_WIDTHS = (N_HEADS_A * 2 * DIFF_QK_DIM, N_HEADS_A * 2 * DIFF_QK_DIM, WIDTH_A,
             WIDTH_B, WIDTH_B, WIDTH_B, WIDTH_C, WIDTH_C)
D_IN = 2816
ROPE_THETA = 500000.0
ROPE_DIM = DIFF_QK_DIM // 4
MAX_POS_OFFSET = 1024
MEM_LEN = 256
CROSS_HEADS = 4
CROSS_DIM = 64
CROSS_WIDTH = CROSS_HEADS * CROSS_DIM
N_EXPERT_GROUPS = 4
EXPERTS_PER_GROUP = 4
N_EXPERTS = N_EXPERT_GROUPS * EXPERTS_PER_GROUP
TOP_K_IN_GROUP = 2
D_EXPERT = 512
EPS = 1e-6

kernel_name = "hybrid_diff_stickbreak_sgu_hmoe"

def rmsnorm(x, g):
    xf = x.astype(jnp.float32)
    y = xf * lax.rsqrt(jnp.mean(xf * xf, axis=-1, keepdims=True) + EPS)
    return (y * g.astype(jnp.float32)).astype(x.dtype)

def rotary_tables(positions):
    inv_freq = ROPE_THETA ** (-jnp.arange(0, ROPE_DIM, 2, dtype=jnp.float32) / ROPE_DIM)
    ang = positions.astype(jnp.float32)[..., None] * inv_freq
    return jnp.cos(ang)[:, :, None, None, :], jnp.sin(ang)[:, :, None, None, :]

def partial_rotary(t, cos, sin):
    half = ROPE_DIM // 2
    t1 = t[..., :half].astype(jnp.float32)
    t2 = t[..., half:ROPE_DIM].astype(jnp.float32)
    rot = jnp.concatenate([t1 * cos - t2 * sin, t2 * cos + t1 * sin], axis=-1).astype(t.dtype)
    return jnp.concatenate([rot, t[..., ROPE_DIM:]], axis=-1)

def diff_attention(q, k, v, lam, subln_g, lam_init):
    B, S, H, _, Dm = q.shape
    nb = S // QBLOCK
    qb = q.reshape(B, nb, QBLOCK, H, 2, Dm).transpose(1, 0, 3, 4, 2, 5)
    kt = k.transpose(0, 2, 3, 1, 4)
    vt = v.transpose(0, 2, 1, 3)
    key_pos = jnp.arange(S)
    scale = Dm ** -0.5

    def block(args):
        qi, start = args
        s = jnp.einsum('bhmqd,bhmkd->bhmqk', qi, kt).astype(jnp.float32) * scale
        qpos = start + jnp.arange(QBLOCK)
        causal = key_pos[None, :] <= qpos[:, None]
        p = jax.nn.softmax(jnp.where(causal, s, -jnp.inf), axis=-1)
        a = p[:, :, 0] - lam * p[:, :, 1]
        return jnp.einsum('bhqk,bhkd->bhqd', a.astype(vt.dtype), vt)

    o = lax.map(block, (qb, jnp.arange(nb) * QBLOCK))
    o = o.transpose(1, 0, 3, 2, 4).reshape(B, S, H, v.shape[-1])
    o = rmsnorm(o, subln_g) * (1.0 - lam_init)
    return o.reshape(B, S, H * v.shape[-1])

def stick_breaking(q, k, v):
    B, S, H, D = q.shape
    nb = S // QBLOCK
    qb = q.reshape(B, nb, QBLOCK, H, D).transpose(1, 0, 3, 2, 4)
    kt = k.transpose(0, 2, 1, 3)
    vt = v.transpose(0, 2, 1, 3)
    key_pos = jnp.arange(S)
    scale = D ** -0.5

    def block(args):
        qi, start = args
        z = jnp.einsum('bhqd,bhkd->bhqk', qi, kt).astype(jnp.float32) * scale
        qpos = start + jnp.arange(QBLOCK)
        strict = key_pos[None, :] < qpos[:, None]
        log_keep = jnp.where(strict, jax.nn.log_sigmoid(-z), 0.0)
        after = lax.cumsum(log_keep, axis=3, reverse=True) - log_keep
        w = jnp.where(strict, jnp.exp(jax.nn.log_sigmoid(z) + after), 0.0)
        return jnp.einsum('bhqk,bhkd->bhqd', w.astype(vt.dtype), vt)

    o = lax.map(block, (qb, jnp.arange(nb) * QBLOCK))
    return o.transpose(1, 0, 3, 2, 4).reshape(B, S, H, D)

def chunk_spatial_gating(u, v, sgu_g, w_s, b_s):
    B, S, _ = v.shape
    nc = S // CHUNK
    vn = rmsnorm(v.reshape(B, S, N_GROUPS_C, SGU_DIM), sgu_g.reshape(N_GROUPS_C, SGU_DIM))
    vc = vn.reshape(B, nc, CHUNK, N_GROUPS_C, SGU_DIM)
    causal = jnp.tril(jnp.ones((CHUNK, CHUNK), dtype=bool))
    ws = jnp.where(causal[None], w_s, 0.0)
    s = jnp.einsum('gts,bnsgc->bntgc', ws, vc) + b_s.T[None, None, :, :, None]
    out = u.reshape(B, nc, CHUNK, N_GROUPS_C, SGU_DIM) * s
    return out.reshape(B, S, N_GROUPS_C, SGU_DIM)

def memory_cross_attention(h, m, w_cq, w_ck, w_cv, w_co):
    B, S, _ = h.shape
    M = m.shape[1]
    q = (h @ w_cq).reshape(B, S, CROSS_HEADS, CROSS_DIM)
    k = (m @ w_ck).reshape(B, M, CROSS_HEADS, CROSS_DIM)
    v = (m @ w_cv).reshape(B, M, CROSS_HEADS, CROSS_DIM)
    s = jnp.einsum('bqhd,bkhd->bhqk', q, k).astype(jnp.float32) * (CROSS_DIM ** -0.5)
    p = jax.nn.softmax(s, axis=-1).astype(v.dtype)
    o = jnp.einsum('bhqk,bkhd->bqhd', p, v).reshape(B, S, CROSS_WIDTH)
    return o @ w_co

def hierarchical_moe(h, w_group, b_group, w_router, b_router, w_gate, w_up, w_down):
    B, S, _ = h.shape
    gl = (h @ w_group).astype(jnp.float32) + b_group.astype(jnp.float32)
    gp = jax.nn.softmax(gl, axis=-1)
    _, gidx = lax.top_k(gl, 1)
    p_group = jnp.take_along_axis(gp, gidx, axis=-1)
    el = ((h @ w_router).astype(jnp.float32) + b_router.astype(jnp.float32)).reshape(
        B, S, N_EXPERT_GROUPS, EXPERTS_PER_GROUP)
    sel = jnp.broadcast_to(gidx[..., None], (B, S, 1, EXPERTS_PER_GROUP))
    el_sel = jnp.take_along_axis(el, sel, axis=2)[:, :, 0, :]
    ev, eidx = lax.top_k(el_sel, TOP_K_IN_GROUP)
    w_sel = jax.nn.softmax(ev, axis=-1) * p_group
    expert_ids = gidx * EXPERTS_PER_GROUP + eidx
    gates = jnp.sum(jax.nn.one_hot(expert_ids, N_EXPERTS, dtype=jnp.float32) * w_sel[..., None], axis=2)
    gates = gates.astype(h.dtype)
    y = jnp.zeros_like(h)
    for e in range(N_EXPERTS):
        act = jax.nn.silu(h @ w_gate[e]) * (h @ w_up[e])
        y = y + gates[..., e:e + 1] * (act @ w_down[e])
    return y

def setup_inputs(seed: int = 0) -> dict:
    key = jax.random.key(seed)
    ks = jax.random.split(key, 40)
    cnt = [0]

    def nk():
        cnt[0] += 1
        return ks[cnt[0] - 1]

    def nrm(shape, scale):
        return jax.random.normal(nk(), shape, jnp.float32) * scale

    def gain(shape):
        return 1.0 + 0.02 * jax.random.normal(nk(), shape, jnp.float32)

    L, D = DEPTH, D_MODEL
    x = nrm((BATCH, SEQ, D), 1.0)
    mem = nrm((BATCH, MEM_LEN, D), 1.0)
    positions = (jax.random.randint(nk(), (BATCH, 1), 0, MAX_POS_OFFSET, dtype=jnp.int32)
                 + jnp.arange(SEQ, dtype=jnp.int32)[None, :])
    return {
        "x": x,
        "mem": mem,
        "positions": positions,
        "norm_mix": gain((L, D)),
        "w_in": nrm((L, D, D_IN), D ** -0.5),
        "lam_q1": nrm((L, DIFF_QK_DIM), 0.1),
        "lam_k1": nrm((L, DIFF_QK_DIM), 0.1),
        "lam_q2": nrm((L, DIFF_QK_DIM), 0.1),
        "lam_k2": nrm((L, DIFF_QK_DIM), 0.1),
        "subln_a": gain((L, DIFF_V_DIM)),
        "norm_b_out": gain((L, WIDTH_B)),
        "sgu_norm": gain((L, WIDTH_C)),
        "w_spatial": nrm((L, N_GROUPS_C, CHUNK, CHUNK), CHUNK ** -0.5),
        "b_spatial": gain((L, N_GROUPS_C, CHUNK)),
        "norm_c_out": gain((L, WIDTH_C)),
        "w_out": nrm((L, D_MIX, D), D_MIX ** -0.5),
        "norm_cross": gain((L, D)),
        "norm_mem": gain((L, D)),
        "w_cq": nrm((L, D, CROSS_WIDTH), D ** -0.5),
        "w_ck": nrm((L, D, CROSS_WIDTH), D ** -0.5),
        "w_cv": nrm((L, D, CROSS_WIDTH), D ** -0.5),
        "w_co": nrm((L, CROSS_WIDTH, D), CROSS_WIDTH ** -0.5),
        "norm_ffn": gain((L, D)),
        "w_group": nrm((L, D, N_EXPERT_GROUPS), D ** -0.5),
        "b_group": nrm((L, N_EXPERT_GROUPS), 0.01),
        "w_router": nrm((L, D, N_EXPERTS), D ** -0.5),
        "b_router": nrm((L, N_EXPERTS), 0.01),
        "w_gate": nrm((L, N_EXPERTS, D, D_EXPERT), D ** -0.5),
        "w_up": nrm((L, N_EXPERTS, D, D_EXPERT), D ** -0.5),
        "w_down": nrm((L, N_EXPERTS, D_EXPERT, D), D_EXPERT ** -0.5),
        "norm_final": gain((D,)),
    }

def reference(x, mem, positions, norm_mix, w_in, lam_q1, lam_k1, lam_q2, lam_k2, subln_a,
              norm_b_out, sgu_norm, w_spatial, b_spatial, norm_c_out, w_out, norm_cross, norm_mem,
              w_cq, w_ck, w_cv, w_co, norm_ffn, w_group, b_group, w_router, b_router,
              w_gate, w_up, w_down, norm_final):
    B, S, _ = x.shape
    cos, sin = rotary_tables(positions)
    split_at = np.cumsum(IN_WIDTHS)[:-1].tolist()
    for l in range(DEPTH):
        lam_init = 0.8 - 0.6 * math.exp(-0.3 * l)
        h = rmsnorm(x, norm_mix[l])
        proj = h @ w_in[l]
        aq, ak, av, bq, bk, bv, cu, cv = jnp.split(proj, split_at, axis=-1)
        aq = partial_rotary(aq.reshape(B, S, N_HEADS_A, 2, DIFF_QK_DIM), cos, sin)
        ak = partial_rotary(ak.reshape(B, S, N_HEADS_A, 2, DIFF_QK_DIM), cos, sin)
        av = av.reshape(B, S, N_HEADS_A, DIFF_V_DIM)
        lam = (jnp.exp(jnp.sum(lam_q1[l].astype(jnp.float32) * lam_k1[l].astype(jnp.float32)))
               - jnp.exp(jnp.sum(lam_q2[l].astype(jnp.float32) * lam_k2[l].astype(jnp.float32)))
               + lam_init)
        ya = diff_attention(aq, ak, av, lam, subln_a[l], lam_init)
        yb = stick_breaking(bq.reshape(B, S, N_HEADS_B, SB_DIM), bk.reshape(B, S, N_HEADS_B, SB_DIM),
                            bv.reshape(B, S, N_HEADS_B, SB_DIM))
        yb = rmsnorm(yb, norm_b_out[l].reshape(N_HEADS_B, SB_DIM)).reshape(B, S, WIDTH_B)
        yc = chunk_spatial_gating(jax.nn.gelu(cu), jax.nn.gelu(cv), sgu_norm[l], w_spatial[l], b_spatial[l])
        yc = rmsnorm(yc, norm_c_out[l].reshape(N_GROUPS_C, SGU_DIM)).reshape(B, S, WIDTH_C)
        mix = jnp.concatenate([ya, yb, yc], axis=-1)
        x = x + mix @ w_out[l]
        x = x + memory_cross_attention(rmsnorm(x, norm_cross[l]), rmsnorm(mem, norm_mem[l]),
                                       w_cq[l], w_ck[l], w_cv[l], w_co[l])
        x = x + hierarchical_moe(rmsnorm(x, norm_ffn[l]), w_group[l], b_group[l], w_router[l],
                                 b_router[l], w_gate[l], w_up[l], w_down[l])
    return rmsnorm(x, norm_final)


_drawn_inputs = setup_inputs


def setup_inputs(seed=0):
    import zlib

    import numpy as np

    out = dict(_drawn_inputs(seed))
    spreads = {}
    factors = {'sgu_norm': 3.541,
     'b_spatial': 3.518,
     'norm_cross': 6.488,
     'norm_mem': 3.68,
     'b_group': 9.495,
     'b_router': 5.867,
     'norm_final': 7.677,
     'norm_ffn': 2.843}
    for name, (base, spread) in spreads.items():
        noise = np.random.default_rng([zlib.crc32(name.encode()), seed]).standard_normal(out[name].shape)
        drawn = base * np.exp(spread * noise) if base else spread * noise
        out[name] = __import__('jax').numpy.asarray(drawn.astype(out[name].dtype))
    for name, factor in factors.items():
        out[name] = (out[name] * factor).astype(out[name].dtype)
    return out
```

```python
import math
from contextlib import ExitStack

import numpy as np

import concourse.bass as bass
from concourse import mybir

F32, BF16, I32 = mybir.dt.float32, mybir.dt.bfloat16, mybir.dt.int32
ALU, ACT, AX = mybir.AluOpType, mybir.ActivationFunctionType, mybir.AxisListType

P = 128
D, S, DEPTH, M = 1024, 512, 2, 256
T, C, MT = S // P, D // P, M // P
H = 4
E, G, F = 16, 4, 512
FC = F // P
EPS = 1e-6
NEG = -1e30
ROPE_THETA, ROPE_DIM = 500000.0, 16
HALF = ROPE_DIM // 2
SLOTS = 6
PW = C * 512
K_V, A_Q, A_K, A_V, B_QK, B_V_C_U, C_V, W_OUT, W_CQ, W_CO, W_EXP = 0, 2, 3, 4, 5, 6, 7, 8, 10, 11, 12
PIECES = W_EXP + 3 * E
assert PIECES % SLOTS == 0
STEPS = T * H + 5
OVER = 3 * E

B_AT = [0, 512, 1024, 896]
B_JOB = [(0, 512), (512, 512), (1024, 256)]
ROWS = {"subln": (0, 128), "b_out": (128, 256), "sgu": (384, 256), "c_out": (640, 256),
        "lam": (896, 256), "route": (1152, G + E)}


class Signal:

    def __init__(self, sem, per_layer=0, unit=1):
        self.sem, self.per_layer, self.unit, self.count = sem, per_layer, unit, 0

    def __call__(self, l, k):
        return self.sem, (k + l * self.per_layer) * self.unit


def done(engine, ins, sig):
    ins.then_inc(sig.sem, 1)
    sig.count += 1
    engine.wait_ge(sig.sem, sig.count)


def trunk(nc, x, mem, positions, norm_mix, w_in, lam_q1, lam_k1, lam_q2, lam_k2, subln_a,
          norm_b_out, sgu_norm, w_spatial, b_spatial, norm_c_out, w_out, norm_cross, norm_mem,
          w_cq, w_ck, w_cv, w_co, norm_ffn, w_group, b_group, w_router, b_router,
          w_gate, w_up, w_down, norm_final, out):
    ctx = ExitStack()
    with ctx:
        def sb(name, shape, dt=F32):
            return ctx.enter_context(nc.sbuf_tensor(name, shape, dt))

        def sem(name):
            return ctx.enter_context(nc.semaphore(name))

        ring = sb("ring", [P, SLOTS, PW])
        X = sb("X", [P, T, D])
        hT = sb("hT", [P, C, S])
        xn = sb("xn", [P, T, D])
        work = sb("work", [P, 11264])
        kmT = sb("kmT", [P, 2, M])
        vm = sb("vm", [P, MT, 256])
        wsT = sb("wsT", [P, G, P])
        rows = sb("rows", [P, 1172])
        gains = sb("gains", [P, DEPTH, 4, C])
        wr = sb("wr", [P, C, G + E])
        bsp = sb("bsp", [P, G])
        ident = sb("ident", [P, P])
        ident_b = sb("ident_b", [P, P], BF16)
        causal_b = sb("causal_b", [P, P], BF16)
        strict = sb("strict", [P, P])
        strict_b = sb("strict_b", [P, P], BF16)
        keep = sb("keep", [P, P])
        neg_tri = sb("neg_tri", [P, P])
        neg_one = sb("neg_one", [P, P])
        one_b = sb("one_b", [P, P], BF16)
        st = sb("st", [P, 256])
        cs = sb("cs", [P, 2, T, HALF])
        rt = sb("rt", [P, 512])
        mask_b = sb("mask_b", [P, T, E], BF16)
        iota4 = sb("iota4", [P, 4])
        iotaE = sb("iotaE", [P, E])
        tok_id = sb("tok_id", [P, T], I32)
        pos_list = sb("pos_list", [P, 2 * T], I32)
        pos_y = sb("pos_y", [P, 2 * T], I32)
        gate = sb("gate", [P, 2, T])
        lists = sb("lists", [P, E], I32)
        over = sb("over", [P, 1], I32)
        over_ids = sb("over_ids", [P, 1], I32)
        pos_i = sb("pos_i", [P, T], I32)
        eps_col = sb("eps_col", [P, 1])
        bank = [ctx.enter_context(nc.psum_tensor(f"bank{i}", [P, 512], F32)) for i in range(8)]

        xn_dram = nc.dram_tensor("xn_dram", [S, D], F32).ap()
        y_dram = nc.dram_tensor("y_dram", [E * S, D], F32).ap()
        list_dram = nc.dram_tensor("list_dram", [S * E, 1], I32).ap()
        mh_dram = nc.dram_tensor("mh_dram", [P, C * M], F32).ap()

        def cut(buf, start, *shape):
            n = int(np.prod(shape))
            v = buf[:, start:start + n]
            if len(shape) == 2:
                return v.rearrange("p (a b) -> p a b", a=shape[0])
            if len(shape) == 3:
                return v.rearrange("p (a b c) -> p a b c", a=shape[0], b=shape[1])
            return v

        aT = cut(work, 0, 8, S)
        bT = cut(work, 4096, 4, S)
        av = cut(work, 6144, T, 512)
        bv = cut(work, 8192, T, 256)
        rot = cut(work, 2048, 4, 128)
        cuv = cut(work, 9216, T, 512)
        mhT = cut(work, 0, C, M)
        mg = cut(work, 2048, C, M)
        mraw = cut(work, 9216, MT, D)
        mn = cut(work, 4096, MT, D)
        pa0 = [cut(work, 9216, 512), cut(work, 10240, 512), rt[:, 0:512]]
        pa1 = [cut(work, 9728, 512), cut(work, 10752, 512)]
        h_flat = hT[:, :, :].rearrange("p c s -> p (c s)")
        sp_buf = h_flat[:, 0:1280]
        w_buf = h_flat[:, 1280:2560]
        pT = cut(h_flat, 2560, 2, 512)
        sq = h_flat[:, 3584:4096]
        sq_big = h_flat[:, 0:1024]
        cqT = cut(work, 0, 2, S)
        pc = cut(work, 1024, 2, H, M)
        pcT = cut(work, 3072, 2, 1024)
        oc = cut(work, 5120, 2, 256)
        ocT = cut(work, 5632, 2, S)
        xg = cut(work, 0, 2, D)
        xgT = cut(work, 2048, 2, D)
        sg = cut(work, 4096, 2, F)
        act_ = cut(work, 5120, 2, F)
        actT = cut(work, 6144, 2, F)
        yo = cut(work, 7168, 2, D)
        sq_moe = cut(work, 0, D)
        yg = h_flat
        wsp = cut(rt, 0, G, P)

        def piece(p):
            return ring[:, p % SLOTS, :]

        def stat(i, n=1):
            return st[:, i:i + n]

        R_LOG, R_EG, R_E2, R_OG, R_PG, R_EL, R_TMP, R_O1, R_O2, R_GI, R_I, R_PR, R_W = (
            0, 80, 96, 104, 120, 128, 144, 208, 224, 240, 244, 252, 316)
        SS, SEED, TMP = 0, 16, 32
        MAXA, SUMA = 48, 80
        RLA = 112
        MAXC, SUMC, RLC = 144, 160, 176
        LAM = 192


        def signal(name, per_layer=0, unit=1):
            return Signal(sem(name), per_layer, unit)

        consts_made, eps_made, mh_done = signal("consts_made"), signal("eps_made"), signal("mh_done")
        wr_loaded = signal("wr_loaded", 3, 16)
        x_loaded, mem_loaded, pos_loaded = signal("x_loaded", unit=16), signal("mem_loaded", unit=16), signal("pos_loaded", unit=16)
        list_cleared = signal("list_cleared", unit=16)
        piece_loaded = [signal(f"piece_loaded_{i}", PIECES // SLOTS, 16) for i in range(SLOTS)]
        act_step, dve_step = signal("act_step"), signal("dve_step")
        angles, rope = signal("angles"), signal("rope")
        mem_seed, mem_norm, mem_tp = signal("mem_seed"), signal("mem_norm"), signal("mem_tp")
        mh_stored, mh_loaded = signal("mh_stored", 0, 16), signal("mh_loaded", 1, 16)
        rows_loaded = signal("rows_loaded", 11, 16)
        gains_loaded = signal("gains_loaded", 4 * DEPTH, 16)
        norm_seed = {n: signal(f"norm_{n}_seed", 1) for n in ("mix", "cross", "ffn")}
        norm_xn = {n: signal(f"norm_{n}_xn", T) for n in norm_seed}
        norm_tp = {n: signal(f"norm_{n}_tp", C) for n in norm_seed}
        norm_act = {n: signal(f"norm_{n}_act", C // 2) for n in norm_seed}
        norm_dve = {n: signal(f"norm_{n}_dve", C // 2) for n in norm_seed}
        mg_ready, kv, k_out, v_out = signal("mg_ready", 1), signal("kv", 4), signal("k_out", 2), signal("v_out", 2)
        proj, proj_act, proj_dve = signal("proj", 24), signal("proj_act", 20), signal("proj_dve", 8)
        rotated, a_tr, aT_act, aT_dve = signal("rotated", T), signal("a_tr", 8), signal("aT_act", 4), signal("aT_dve", 4)
        ws_tr, ws_ready, c_mm, c_out = signal("ws_tr", 1), signal("ws_ready", 1), signal("c_mm", 2), signal("c_out", 2)
        g_sq, g_ss, g_seed, g_out = (signal(n, 7) for n in ("g_sq", "g_ss", "g_seed", "g_out"))
        lam_sum, lam_exp, lam_ready = signal("lam_sum", 1), signal("lam_exp", 1), signal("lam_ready", 1)
        U = T * H
        a_scores, a_max, a_exp, a_comb = signal("a_scores", U), signal("a_max", U), signal("a_exp", 2 * U), signal("a_comb", U)
        a_tp, a_pt, a_pv, a_out = signal("a_tp", U), signal("a_pt", U), signal("a_pv", U), signal("a_out", T)
        b_z, b_min, b_ln, b_sp = signal("b_z", 3 * H), signal("b_min", 3 * H), signal("b_ln", 3 * H), signal("b_sp", H)
        b_sfx, b_w, b_wm, b_pv, b_out = signal("b_sfx", 3 * H), signal("b_w", 3 * H), signal("b_wm", H), signal("b_pv", H), signal("b_out", H)
        mix_tp, mixT_act, mixT_dve = signal("mix_tp", C), signal("mixT_act", 4), signal("mixT_dve", 4)
        o_mm, x_mix = signal("o_mm", 8), signal("x_mix", 8)
        cq, cq_out = signal("cq", 2), signal("cq_out", 2)
        c_scores, c_max, c_exp = signal("c_scores", T), signal("c_max", T), signal("c_exp", T)
        c_tp, c_pt_act, c_pt_dve, c_pv, c_o = signal("c_tp", 2 * T), signal("c_pt_act", T), signal("c_pt_dve", T), signal("c_pv", T), signal("c_o", T)
        c_otp, c_ot, co_mm, x_cross = signal("c_otp", T), signal("c_ot", T), signal("co_mm", 8), signal("x_cross", 8)
        xn_stored, logits, r_max, r_exp, masks = signal("xn_stored", 1, 16), signal("logits", 1), signal("r_max", 2), signal("r_exp", 2), signal("masks", 1)
        ranks, pos_ready, scattered, lists_loaded = signal("ranks", 1), signal("pos_ready", 1), signal("scattered", 8, 16), signal("lists_loaded", 1, 16)
        gathered = [signal(f"gathered_{i}", E // 2, 16) for i in range(2)]
        xg_tp, xg_out, gate_up, sig_exp, act_ready = signal("xg_tp", 2 * E), signal("xg_out", 2 * E), signal("gate_up", E), signal("sig_exp", E), signal("act_ready", E)
        gate_done = signal("gate_done", E)
        silu_step = signal("silu_step", 3 * E)
        act_tp, actT_out, down, y_out = signal("act_tp", E), signal("actT_out", E), signal("down", 2 * E), signal("y_out", 2 * E)
        y_stored = [signal(f"y_stored_{i}", E // 2, 16) for i in range(2)]
        over_w = [signal(f"over_w_{l}", unit=16) for l in range(DEPTH)]
        over_ids_in = [signal(f"over_ids_in_{l}", unit=16) for l in range(DEPTH)]
        over_go = [signal(f"over_go_{l}") for l in range(DEPTH)]
        over_x = [signal(f"over_x_{l}", unit=16) for l in range(DEPTH)]
        over_y = [signal(f"over_y_{l}", unit=16) for l in range(DEPTH)]
        over_pe = [signal(f"over_pe_{l}") for l in range(DEPTH)]
        over_act = [signal(f"over_act_{l}") for l in range(DEPTH)]
        over_dve = [signal(f"over_dve_{l}") for l in range(DEPTH)]
        pair_loaded = [signal(f"pair_loaded_{i}", 2, 16) for i in range(4)]
        x_moe, out_ready, out_stored = signal("x_moe", 2 * T), signal("out_ready"), signal("out_stored", unit=16)

        y_first = y_dram[0:E * P, :].rearrange("(e s) d -> e s d", e=E)
        y_over = y_dram[E * P:E * S, :].rearrange("(e r s) d -> e r s d", e=E, r=3)

        block = ctx.enter_context(nc.Block())

        @block.sync
        def _(sp):
            def used(l, q):
                if q < W_EXP:
                    return {K_V: kv(l, 2), K_V + 1: kv(l, 4), W_OUT: o_mm(l, 4), W_OUT + 1: o_mm(l, 8),
                            W_CQ: cq(l, 2), W_CO: co_mm(l, 8)}.get(q) or proj(l, 4 * (q - A_Q + 1))
                q -= W_EXP
                if q in (0, 1):
                    return (gate_done, gate_up)[q](l, 1)
                if q == 3 * E - 1:
                    return down(l, 2 * E)
                i = (q + 1) // 3
                return (gate_done(l, i + 1), gate_up(l, i + 1), down(l, 2 * i))[(q + 1) % 3]

            def load(p, dst, src, wait=True):
                if p >= SLOTS and wait:
                    sp.wait_ge(*used((p - SLOTS) // PIECES, (p - SLOTS) % PIECES))
                sp.dma_start(dst, src).then_inc(piece_loaded[p % SLOTS].sem, 16)

            def wide(p, n):
                return piece(p)[:, 0:C * n].rearrange("p (c n) -> p c n", n=n)

            def columns(w, a, n):
                return w[:, a:a + n].rearrange("(p c) n -> p c n", c=C)

            for t in range(T):
                sp.dma_start(X[:, t, :], x[0, t * P:(t + 1) * P, :]).then_inc(x_loaded.sem, 16)
            for l in range(DEPTH):
                b = l * PIECES
                load(b + K_V, wide(b + K_V, 256), columns(w_ck[l], 0, 256))
                load(b + K_V + 1, wide(b + K_V + 1, 256), columns(w_cv[l], 0, 256))
                for n in range(5):
                    load(b + A_Q + n, wide(b + A_Q + n, 512), columns(w_in[l], 512 * n, 512))
                load(b + C_V, wide(b + C_V, 256), columns(w_in[l], 2560, 256))
                for n in range(2):
                    load(b + W_OUT + n, wide(b + W_OUT + n, 512), columns(w_out[l], 512 * n, 512))
                load(b + W_CQ, wide(b + W_CQ, 256), columns(w_cq[l], 0, 256))
                load(b + W_CO, piece(b + W_CO)[:, 0:2 * D], w_co[l].rearrange("(p c) n -> p (c n)", c=2))
                gate_v = w_gate[l].rearrange("e (p c) f -> e p (c f)", c=C)
                up_v = w_up[l].rearrange("e (p c) f -> e p (c f)", c=C)
                down_v = w_down[l].rearrange("e (p c) n -> e p (c n)", c=FC)

                def expert(i):
                    p = b + W_EXP + (3 * i - 1 if i else 0)
                    load(p, piece(p), gate_v[i])
                    load(p + 1, piece(p + 1), up_v[i])
                    if i:
                        load(p + 2, piece(p + 2), down_v[i - 1])

                def expert_in_loop(k, a):
                    i, p = 2 * k + a, W_EXP + 3 * a - 1
                    sp.wait_ge(*gate_done(l, i - 1))
                    load(p, piece(p), gate_v[i], False)
                    sp.wait_ge(*gate_up(l, i - 1))
                    load(p + 1, piece(p + 1), up_v[i], False)
                    sp.wait_ge(*down(l, 2 * i - 4))
                    load(p + 2, piece(p + 2), down_v[i - 1], False)

                for i in range(3):
                    expert(i)
                with sp.Fori(0, 6) as k:
                    expert_in_loop(k, 3)
                    expert_in_loop(k, 4)
                expert(15)
                p = b + PIECES - 1
                load(p, piece(p), down_v[E - 1])
                sp.wait_ge(*pos_ready(l, 1))
                more = sp.value_load(over[0:1, 0:1], min_val=0, max_val=1)
                with sp.If(more > 0):
                    sp.wait_ge(*down(l, 2 * E))
                    with sp.Fori(0, E) as e:
                        with sp.Fori(0, 3) as r:
                            sp.wait_ge(over_pe[l].sem, e * 15 + r * 5 + 1)
                            for n, w in enumerate((gate_v, up_v, down_v)):
                                sp.dma_start(ring[:, n, :], w[e]).then_inc(over_w[l].sem, 16)
                    sp.wait_ge(*over_w[l](0, 3 * OVER))
                    sp.wait_ge(*over_pe[l](0, 5 * OVER + 1))
                sp.end_ifs()

        @block.gpsimd
        def _(pool):
            def const(ins):
                done(pool, ins, consts_made)

            for m, v in ((ident, 0.0), (ident_b, 0.0), (causal_b, 0.0), (strict, 1.0), (strict_b, 1.0),
                         (keep, 1.0), (neg_tri, -1.0), (neg_one, -1.0), (one_b, 1.0)):
                const(nc.gpsimd.memset(m[:, :], v))

            def select(m, op, fill, base, cm, step):
                const(nc.gpsimd.affine_select(out=m[:, :], in_=m[:, :], compare_op=op, fill=fill, base=base,
                                              pattern=[[step, P]], channel_multiplier=cm))

            select(ident, ALU.not_equal, 1.0, 0, 1, -1)
            select(ident_b, ALU.not_equal, 1.0, 0, 1, -1)
            pool.dma_start(pos_i[:, :], positions[0].rearrange("(t p) -> p t", p=P),
                           allow_slow_non_contiguous=True).then_inc(pos_loaded.sem, 16)
            pool.dma_start(mraw[:, :, :], mem[0].rearrange("(t p) d -> p t d", p=P)).then_inc(mem_loaded.sem, 16)
            for l in range(DEPTH):
                for n, g in enumerate((norm_mix, norm_cross, norm_ffn, norm_mem)):
                    pool.dma_start(gains[:, l, n, :], g[l].rearrange("(p c) -> p c", c=C)).then_inc(gains_loaded.sem, 16)
            select(causal_b, ALU.is_ge, NEG, 0, 1, -1)
            select(strict, ALU.is_gt, 0.0, 0, -1, 1)
            select(strict_b, ALU.is_gt, 0.0, 0, -1, 1)
            select(keep, ALU.is_ge, 0.0, 0, -1, 1)
            select(neg_tri, ALU.is_ge, 0.0, 0, 1, -1)
            const(nc.gpsimd.iota(tok_id[:, :], pattern=[[P, T]], base=0, channel_multiplier=1))
            const(nc.gpsimd.iota(iota4[:, :], pattern=[[1, 4]], base=0, channel_multiplier=0,
                                 allow_small_or_imprecise_dtypes=True))
            const(nc.gpsimd.iota(iotaE[:, :], pattern=[[1, E]], base=0, channel_multiplier=0,
                                 allow_small_or_imprecise_dtypes=True))
            const(nc.gpsimd.memset(lists[:, :], 0))
            for r in range(T):
                pool.dma_start(list_dram[r * P * E:(r + 1) * P * E, :].rearrange("(s e) o -> s (e o)", e=E),
                               lists[:, :]).then_inc(list_cleared.sem, 16)
            pool.wait_ge(*list_cleared(0, T))

            def combine(l, y):
                pool.wait_ge(*y_stored[0](l, E // 2))
                pool.wait_ge(*y_stored[1](l, E // 2))
                for n in range(2 * T):
                    if n >= 4:
                        pool.wait_ge(*x_moe(l, n - 3))
                    pool.indirect_dma_start(out=yg[:, (n % 4) * D:(n % 4 + 1) * D], out_offset=None, in_=y,
                                            in_offset=bass.IndirectOffsetOnAxis(ap=pos_y[:, n:n + 1], axis=0)
                                            ).then_inc(pair_loaded[n % 4].sem, 16)

            for l in range(DEPTH):
                if l:
                    pool.wait_ge(*logits(l - 1, 1))
                    pool.wait_ge(*ranks(l - 1, 1))
                    pool.wait_ge(*pos_ready(l - 1, 1))
                def row(name, src):
                    a, n = ROWS[name]
                    pool.dma_start(rows[:, a:a + n], src.partition_broadcast(P)).then_inc(rows_loaded.sem, 16)
                for n, v in enumerate((lam_q1, lam_q2, lam_k1, lam_k2)):
                    a = ROWS["lam"][0] + 64 * n
                    pool.dma_start(rows[:, a:a + 64], v[l].partition_broadcast(P)).then_inc(rows_loaded.sem, 16)
                row("subln", subln_a[l])
                row("b_out", norm_b_out[l])
                row("sgu", sgu_norm[l])
                row("c_out", norm_c_out[l])
                a = ROWS["route"][0]
                pool.dma_start(rows[:, a:a + G], b_group[l].partition_broadcast(P)).then_inc(rows_loaded.sem, 16)
                pool.dma_start(rows[:, a + G:a + G + E], b_router[l].partition_broadcast(P)).then_inc(rows_loaded.sem, 16)
                pool.dma_start(bsp[:, :], b_spatial[l].rearrange("g t -> t g"),
                               allow_slow_non_contiguous=True).then_inc(rows_loaded.sem, 16)
                pool.dma_start(wr[:, :, 0:G], w_group[l].rearrange("(p c) g -> p c g", c=C)).then_inc(wr_loaded.sem, 16)
                pool.dma_start(wr[:, :, G:G + E], w_router[l].rearrange("(p c) g -> p c g", c=C)).then_inc(wr_loaded.sem, 16)
                pool.dma_start(wsp[:, :, :], w_spatial[l].rearrange("g t s -> t g s")).then_inc(wr_loaded.sem, 16)
                if l == 0:
                    pool.wait_ge(*mh_done(0, 4))
                    pool.dma_start(mh_dram[:, :], mhT[:, :, :].rearrange("p c m -> p (c m)")).then_inc(mh_stored.sem, 16)
                    pool.wait_ge(*mh_stored(0, 1))
                else:
                    pool.wait_ge(*y_stored[0](l - 1, E // 2))
                    pool.wait_ge(*y_stored[1](l - 1, E // 2))
                    pool.wait_ge(*x_moe(l - 1, 2 * T))
                    pool.dma_start(mhT[:, :, :].rearrange("p c m -> p (c m)"), mh_dram[:, :]).then_inc(mh_loaded.sem, 16)

                pool.wait_ge(*norm_xn["ffn"](l, T))
                pool.dma_start(xn_dram[:, :].rearrange("(t p) d -> p t d", p=P), xn[:, :, :]).then_inc(xn_stored.sem, 16)
                pool.wait_ge(*pos_ready(l, 1))
                for n in range(2 * T):
                    pool.indirect_dma_start(out=list_dram[:, :], out_offset=bass.IndirectOffsetOnAxis(ap=pos_list[:, n:n + 1], axis=0),
                                            in_=tok_id[:, n // 2:n // 2 + 1], in_offset=None).then_inc(scattered.sem, 16)
                pool.wait_ge(*scattered(l, 2 * T))
                pool.dma_start(lists[:, :], list_dram[0:P * E, :].rearrange("(s e) o -> s (e o)", e=E)).then_inc(lists_loaded.sem, 16)
                pool.wait_ge(*lists_loaded(l, 1))
                pool.wait_ge(*xn_stored(l, 1))
                pool.wait_ge(*x_cross(l, 8))

                for e in range(E):
                    if e >= 2:
                        pool.wait_ge(*xg_tp(l, 2 * (e - 1)))
                    pool.indirect_dma_start(out=xg[:, e % 2, :], out_offset=None, in_=xn_dram[:, :],
                                            in_offset=bass.IndirectOffsetOnAxis(ap=lists[:, e:e + 1], axis=0)
                                            ).then_inc(gathered[e % 2].sem, 16)
                more = pool.value_load(over[0:1, 0:1], min_val=0, max_val=1)
                with pool.If(more > 0):
                    pool.wait_ge(*y_stored[0](l, E // 2))
                    pool.wait_ge(*y_stored[1](l, E // 2))
                    with pool.Fori(0, E) as e:
                        with pool.Fori(0, 3) as r:
                            pool.wait_ge(over_pe[l].sem, e * 15 + r * 5 + 1)
                            src = list_dram.rearrange("(r s e) o -> e r s o", r=T, e=E)
                            pool.dma_start(over_ids[:, :], src[e, r + 1],
                                           allow_slow_non_contiguous=True).then_inc(over_ids_in[l].sem, 16)
                            pool.wait_ge(over_ids_in[l].sem, e * 48 + r * 16 + 16)
                            pool.sem_inc(over_go[l].sem, 1)
                            pool.indirect_dma_start(out=xg[:, 0, :], out_offset=None, in_=xn_dram[:, :],
                                                    in_offset=bass.IndirectOffsetOnAxis(ap=over_ids[:, 0:1], axis=0)
                                                    ).then_inc(over_x[l].sem, 16)
                    pool.wait_ge(*over_y[l](0, OVER))
                    combine(l, y_dram[:, :])
                with pool.Else():
                    combine(l, y_dram[0:E * P, :])
                pool.end_ifs()
            pool.wait_ge(*pos_ready(DEPTH - 1, 1))
            pool.dma_start(rows[:, 0:D], norm_final.partition_broadcast(P)).then_inc(rows_loaded.sem, 16)

        @block.scalar
        def _(act):
            def step(ins):
                done(act, ins, act_step)

            def rstd_seed(n, width, sig):
                step(nc.scalar.activation(stat(SEED, n), stat(SS, n), ACT.Ln, bias=eps_col[:, :], scale=1.0 / width))
                done(act, nc.scalar.activation(stat(SEED, n), stat(SEED, n), ACT.Exp, scale=-0.5), sig)

            def norm(l, name, arrived):
                for t in range(T):
                    arrived(t)
                    ins = nc.scalar.activation(xn[:, t, :], X[:, t, :], ACT.Square, accum_out=stat(SS + t))
                    step(ins)
                rstd_seed(T, D, norm_seed[name])

            def norm_evac(l, name, g):
                for c in range(0, C, 2):
                    act.wait_ge(*norm_tp[name](l, c + 1))
                    done(act, nc.scalar.activation(hT[:, c, :], bank[c][:, :], ACT.Copy, scale=gains[:, l, g, c:c + 1]), norm_act[name])

            def group_norm(l, k, src, tmp, n, width):
                done(act, nc.scalar.activation(tmp, src, ACT.Square), g_sq)
                act.wait_ge(*g_ss(l, k + 1))
                rstd_seed(n, width, g_seed)

            act.wait_ge(*angles(0, 1))
            done(act, nc.scalar.activation(cs[:, :, :, :], cs[:, :, :, :], ACT.Sin), rope)
            nc.scalar.preload_act_table_set("natural_log_exp_and_others")
            act.wait_ge(*mem_loaded(0, 1))
            for t in range(MT):
                step(nc.scalar.activation(mn[:, t, :], mraw[:, t, :], ACT.Square, accum_out=stat(SS + t)))
            act.wait_ge(*eps_made(0, 1))
            rstd_seed(MT, D, mem_seed)

            for l in range(DEPTH):
                if l == 0:
                    act.wait_ge(*mem_norm(0, MT))
                    act.wait_ge(*x_loaded(0, T))
                    norm(l, "mix", lambda t: None)
                else:
                    act.wait_ge(*xn_stored(l - 1, 1))
                    norm(l, "mix", lambda t: act.wait_ge(*x_moe(l - 1, 2 * t + 2)))
                if l == 0:
                    act.wait_ge(*gains_loaded(0, 4 * DEPTH))
                for j in range(2):
                    act.wait_ge(*kv(l, j + 1))
                    done(act, nc.scalar.activation(kmT[:, j, :], bank[j][:, 0:M], ACT.Copy), k_out)
                norm_evac(l, "mix", 0)

                for j in range(8):
                    act.wait_ge(*proj(l, j + 1))
                    t, n = j % T, j // T
                    done(act, nc.scalar.activation(xn[:, t, 512 * n:512 * n + 512], bank[j][:, :], ACT.Copy), proj_act)
                for j in range(4):
                    act.wait_ge(*proj(l, 12 + j + 1))
                    done(act, nc.scalar.activation(bT[:, j, :], bank[4 + j][:, :], ACT.Copy,
                                                   scale=0.125 if j < 2 else 1.0), proj_act)
                for t in range(T):
                    act.wait_ge(*proj_dve(l, 4 + t + 1))
                    done(act, nc.scalar.activation(cuv[:, t, 0:256], bank[t][:, 256:512], ACT.Gelu_apprx_tanh), proj_act)
                for t in range(T):
                    act.wait_ge(*proj(l, 20 + t + 1))
                    done(act, nc.scalar.activation(cuv[:, t, 256:512], bank[4 + t][:, 0:256], ACT.Gelu_apprx_tanh), proj_act)
                nc.scalar.preload_act_table_set("natural_log_exp_and_others")
                if l == 0:
                    act.wait_ge(*mh_stored(0, 1))
                for cc in range(0, 8, 2):
                    act.wait_ge(*a_tr(l, cc + 1))
                    done(act, nc.scalar.activation(aT[:, cc, :], bank[cc][:, :], ACT.Copy), aT_act)
                group_norm(l, 0, cuv[:, :, 256:512], sq_big.rearrange("p (t n) -> p t n", t=T), 16, 64)
                act.wait_ge(*lam_sum(l, 1))
                done(act, nc.scalar.activation(stat(LAM + 2, 2), stat(LAM, 2), ACT.Exp), lam_exp)
                act.wait_ge(*c_out(l, 2))
                group_norm(l, 1, xn[:, :, 768:1024], sq_big.rearrange("p (t n) -> p t n", t=T), 16, 64)

                def a_step(i):
                    if i < U:
                        t, n = i // H, P * (i // H + 1)
                        act.wait_ge(*a_max(l, i + 1))
                        if i >= 3:
                            act.wait_ge(*a_tp(l, i - 2))
                        for m in range(2):
                            o = pa1[i % 2] if m else pa0[i % 3]
                            done(act, nc.scalar.activation(o[:, 0:n], bank[(2 * i + m) % 3][:, 0:n], ACT.Exp,
                                                           bias=stat(MAXA + 2 * i + m), scale=0.125,
                                                           accum_out=stat(SUMA + 2 * i + m)), a_exp)
                    u = i - 2
                    if 0 <= u < U:
                        n = P * (u // H + 1)
                        act.wait_ge(*a_tp(l, u + 1))
                        if u >= 2:
                            act.wait_ge(*a_pv(l, u - 1))
                        done(act, nc.scalar.activation(pT[:, u % 2, 0:n], bank[4][:, 0:n], ACT.Copy), a_pt)

                def a_norm(i):
                    if i >= 7 and (i - 7) % H == 0 and (i - 7) // H < T:
                        t = (i - 7) // H
                        act.wait_ge(*a_out(l, t + 1))
                        done(act, nc.scalar.activation(sq, xn[:, t, 0:512], ACT.Square), g_sq)
                    if i >= 8 and (i - 8) % H == 0 and (i - 8) // H < T:
                        act.wait_ge(*g_ss(l, 3 + (i - 8) // H))
                        rstd_seed(H, P, g_seed)

                def b_step(i):
                    h, part = i // 4, i % 4
                    if h < H and part == 0:
                        for j, (a, n) in enumerate(B_JOB):
                            act.wait_ge(*b_min(l, 3 * h + j + 1))
                            step(nc.scalar.activation(sp_buf[:, a:a + n], sp_buf[:, a:a + n], ACT.Exp))
                            done(act, nc.scalar.activation(sp_buf[:, a:a + n], sp_buf[:, a:a + n], ACT.Ln, bias=1.0), b_ln)
                    if h < H and part == 2:
                        for j, (a, n) in enumerate(B_JOB):
                            act.wait_ge(*b_sfx(l, 3 * h + j + 1))
                            if h and j == 0:
                                act.wait_ge(*b_pv(l, h))
                            done(act, nc.scalar.activation(w_buf[:, a:a + n], bank[(6, 7, 3)[j]][:, 0:n], ACT.Exp), b_w)

                for i in range(STEPS):
                    a_step(i)
                    b_step(i)
                    a_norm(i)
                act.wait_ge(*b_out(l, H))
                group_norm(l, 6, xn[:, :, 512:768], cut(h_flat, 1280, T, 256), 16, 64)

                for c in range(0, C, 2):
                    act.wait_ge(*mix_tp(l, c + 1))
                    done(act, nc.scalar.activation(hT[:, c, :], bank[c][:, :], ACT.Copy), mixT_act)

                norm(l, "cross", lambda t: act.wait_ge(*x_mix(l, 4 + t + 1)))
                norm_evac(l, "cross", 1)
                for j in range(2):
                    act.wait_ge(*cq(l, j + 1))
                    done(act, nc.scalar.activation(cqT[:, j, :], bank[j][:, :], ACT.Copy), cq_out)
                for t in range(T):
                    act.wait_ge(*c_max(l, t + 1))
                    if t >= 2:
                        act.wait_ge(*c_tp(l, 2 * (t - 1)))
                    for h in range(H):
                        ins = nc.scalar.activation(pc[:, t % 2, h, :], bank[2 + 2 * (t % 2) + h % 2][:, (h // 2) * M:(h // 2 + 1) * M],
                                                   ACT.Exp, bias=stat(MAXC + H * t + 2 * (h % 2) + h // 2), scale=0.125, accum_out=stat(SUMC + H * t + h))
                        done(act, ins, c_exp if h == H - 1 else act_step)
                    act.wait_ge(*c_tp(l, 2 * t + 1))
                    if t >= 2:
                        act.wait_ge(*c_pv(l, t - 1))
                    done(act, nc.scalar.activation(pcT[:, t % 2, 0:512], bank[6][:, :], ACT.Copy), c_pt_act)
                    act.wait_ge(*c_otp(l, t + 1))
                    done(act, nc.scalar.activation(ocT[:, :, t * P:(t + 1) * P],
                                                   bank[t % 2][:, 256:512].rearrange("p (c n) -> p c n", c=2), ACT.Copy), c_ot)

                norm(l, "ffn", lambda t: act.wait_ge(*x_cross(l, 2 * t + 2)))
                norm_evac(l, "ffn", 2)
                act.wait_ge(*r_max(l, 1))
                done(act, nc.scalar.activation(cut(rt, R_EG, T, G), cut(rt, R_EG, T, G), ACT.Exp), r_exp)
                act.wait_ge(*r_max(l, 2))
                done(act, nc.scalar.activation(cut(rt, R_E2, T), cut(rt, R_E2, T), ACT.Exp), r_exp)

                def moe_step(k, a, gu=True, dn=True):
                    i = 2 * k + a
                    if dn:
                        act.wait_ge(*act_tp(l, i))
                        nc.scalar.activation(actT[:, (a - 1) % 2, :], bank[7][:, :], ACT.Copy).then_inc(actT_out.sem, 1)
                    if gu:
                        act.wait_ge(*gate_up(l, i + 1))
                        if a >= 2:
                            act.wait_ge(*act_ready(l, i - 1))
                        nc.scalar.activation(sg[:, a % 2, :], bank[2 * (a % 2)][:, :], ACT.Exp, scale=-1.0).then_inc(sig_exp.sem, 1)
                    if dn:
                        s = (a - 1) % 2
                        if a >= 3:
                            act.wait_ge(*y_stored[s](l, k + (a - 1) // 2))
                        for n in range(2):
                            act.wait_ge(*down(l, 2 * i - 1 + n))
                            nc.scalar.activation(yo[:, s, 512 * n:512 * n + 512], bank[4 + n][:, :], ACT.Copy).then_inc(y_out.sem, 1)
                        act.wait_ge(*y_out(l, 2 * i))
                        act.dma_start(y_first[i - 1], yo[:, s, :]).then_inc(y_stored[s].sem, 16)

                
                moe_step(0, 0, dn=False)
                moe_step(0, 1)
                moe_step(0, 2)
                with act.Fori(0, 6) as k:
                    moe_step(k, 3)
                    moe_step(k, 4)
                moe_step(0, 15)
                moe_step(0, 16, gu=False)
                more = act.value_load(over[0:1, 0:1], min_val=0, max_val=1)
                with act.If(more > 0):
                    act.wait_ge(*y_stored[0](l, E // 2))
                    with act.Fori(0, E) as e:
                        with act.Fori(0, 3) as r:
                            n = 3 * e + r
                            oa = over_act[l].sem
                            act.wait_ge(over_pe[l].sem, 5 * n + 1 + 3)
                            nc.scalar.activation(sg[:, 0, :], bank[0][:, :], ACT.Exp, scale=-1.0).then_inc(oa, 1)
                            act.wait_ge(over_pe[l].sem, 5 * n + 1 + 4)
                            nc.scalar.activation(actT[:, 0, :], bank[7][:, :], ACT.Copy).then_inc(oa, 1)
                            act.wait_ge(over_pe[l].sem, 5 * n + 1 + 5)
                            for q in range(2):
                                nc.scalar.activation(yo[:, 0, 512 * q:512 * q + 512], bank[4 + q][:, :], ACT.Copy).then_inc(oa, 1)
                            act.wait_ge(oa, 4 * n + 4)
                            act.dma_start(y_over[e, r], yo[:, 0, :]).then_inc(over_y[l].sem, 16)
                            act.wait_ge(over_y[l].sem, 16 * n + 16)
                act.end_ifs()

            act.wait_ge(*xn_stored(DEPTH - 1, 1))
            norm(DEPTH, "mix", lambda t: act.wait_ge(*x_moe(DEPTH - 1, 2 * t + 2)))
            for t in range(T):
                act.wait_ge(*out_ready(0, t + 1))
                act.dma_start(out[0, t * P:(t + 1) * P, :], X[:, t, :]).then_inc(out_stored.sem, 16)
            act.wait_ge(*out_stored(0, T))

        @block.vector
        def _(dve):
            def step(ins):
                done(dve, ins, dve_step)

            def scale_(o, i, s1, s2=None, op0=ALU.mult, op1=ALU.add):
                return nc.vector.tensor_scalar(o, i, s1, s2, op0, *([] if s2 is None else [op1]))

            def tt(o, a, b, op=ALU.mult):
                return nc.vector.tensor_tensor(o, a, b, op)

            def newton(n, width):
                r, t_ = stat(SEED, n), stat(TMP, n)
                step(scale_(t_, stat(SS, n), 1.0 / width, EPS))
                step(tt(t_, t_, r))
                step(tt(t_, t_, r))
                step(scale_(t_, t_, -0.5, 1.5))
                step(tt(r, r, t_))

            def norm(l, name):
                dve.wait_ge(*norm_seed[name](l, 1))
                newton(T, D)
                for t in range(T):
                    done(dve, scale_(xn[:, t, :], X[:, t, :], stat(SEED + t)), norm_xn[name])

            def norm_evac(l, name, g):
                for c in range(1, C, 2):
                    dve.wait_ge(*norm_tp[name](l, c + 1))
                    done(dve, scale_(hT[:, c, :], bank[c][:, :], gains[:, l, g, c:c + 1]), norm_dve[name])

            def group_sums(l, k, tmp, n):
                dve.wait_ge(*g_sq(l, k + 1))
                done(dve, nc.vector.tensor_reduce(stat(SS, n), tmp, AX.X, ALU.add), g_ss)

            def group_scale(l, k, view, n, width, outer, gain, inner, factor=1.0):
                dve.wait_ge(*g_seed(l, k + 1))
                newton(n, width)
                r = stat(SEED, n)
                if outer:
                    r = r.rearrange("p (t g) -> p t g", t=outer)[:, :, :, None].broadcast_to([P, outer, n // outer, width])
                    step(tt(view, view, r))
                    done(dve, tt(inner, inner, gain[:, None, :].broadcast_to([P, outer, inner.shape[2]])), g_out)
                else:
                    step(tt(view, view, r[:, :, None].broadcast_to([P, n, width])))
                    done(dve, nc.vector.scalar_tensor_tensor(view, view, factor, gain[:, None, :].broadcast_to([P, n, width]),
                                                             ALU.mult, ALU.mult), g_out)

            def row(name):
                a, n = ROWS[name]
                return rows[:, a:a + n]

            done(dve, nc.vector.memset(eps_col[:, :], EPS), eps_made)
            dve.wait_ge(*pos_loaded(0, 1))
            posf = stat(0, T)
            step(nc.vector.tensor_copy(posf, pos_i[:, :]))
            inv = (np.float32(1.0) / np.power(np.float32(ROPE_THETA), np.arange(0, ROPE_DIM, 2, dtype=np.float32) / np.float32(ROPE_DIM))).astype(np.float32)
            ang, turns = cut(rot[:, 0, :], 0, T, HALF), cut(rot[:, 1, :], 0, T, HALF)
            for i in range(HALF):
                step(scale_(ang[:, :, i], posf, float(inv[i])))
            two_pi = 2 * math.pi
            p1 = 6.28125
            p2 = 0.0019350051879882812
            p3 = two_pi - p1 - p2
            magic = 12582912.0
            for w, (off, shift) in enumerate(((0.25, math.pi / 2), (0.0, 0.0))):
                step(scale_(turns, ang, 1 / two_pi, off))
                step(scale_(turns, turns, magic, None, ALU.add))
                step(scale_(turns, turns, magic, None, ALU.subtract))
                o = cs[:, w, :, :]
                step(nc.vector.scalar_tensor_tensor(o, turns, -p1, ang, ALU.mult, ALU.add))
                step(nc.vector.scalar_tensor_tensor(o, turns, -p2, o, ALU.mult, ALU.add))
                step(nc.vector.scalar_tensor_tensor(o, turns, -p3, o, ALU.mult, ALU.add))
                step(scale_(o, o, shift, None, ALU.add))
                done(dve, scale_(o, o, 3.1415925, -3.1415925, ALU.min, ALU.max), angles if w else dve_step)

            dve.wait_ge(*mem_seed(0, 1))
            newton(MT, D)
            for t in range(MT):
                done(dve, scale_(mn[:, t, :], mraw[:, t, :], stat(SEED + t)), mem_norm)
            for j in range(4):
                dve.wait_ge(*mem_tp(0, j + 1))
                done(dve, nc.vector.tensor_copy(cut(work, 512 * j, 512), bank[j][:, :]), mh_done)
            dve.wait_ge(*gains_loaded(0, 4 * DEPTH))

            for l in range(DEPTH):
                if l:
                    dve.wait_ge(*mh_loaded(l - 1, 1))
                else:
                    dve.wait_ge(*mh_done(0, 4))
                done(dve, tt(mg[:, :, :], mhT[:, :, :], gains[:, l, 3, :][:, :, None].broadcast_to([P, C, M])), mg_ready)
                norm(l, "mix")
                for t in range(MT):
                    dve.wait_ge(*kv(l, 2 + t + 1))
                    done(dve, nc.vector.tensor_copy(vm[:, t, :], bank[2 + t][:, 0:256]), v_out)
                norm_evac(l, "mix", 0)
                dve.wait_ge(*rows_loaded(l, 11))
                a = ROWS["lam"][0]
                step(tt(rot[:, 0, :], rows[:, a:a + 128], rows[:, a + 128:a + 256]))
                done(dve, nc.vector.tensor_reduce(stat(LAM, 2), cut(rot[:, 0, :], 0, 2, 64), AX.X, ALU.add), lam_sum)
                if l == 0:
                    dve.wait_ge(*rope(0, 1))
                for t in range(T):
                    dve.wait_ge(*proj_act(l, 4 + t + 1))
                    v = xn[:, t, :].rearrange("p (n d) -> p n d", d=64)
                    lo, hi = v[:, :, 0:HALF], v[:, :, HALF:ROPE_DIM]
                    co = cs[:, 0, t, :][:, None, :].broadcast_to([P, 16, HALF])
                    si = cs[:, 1, t, :][:, None, :].broadcast_to([P, 16, HALF])
                    q = [cut(rot[:, n, :], 0, 16, HALF) for n in range(4)]
                    step(tt(q[0], lo, co))
                    step(tt(q[1], hi, si))
                    step(tt(q[2], hi, co))
                    step(tt(q[3], lo, si))
                    step(tt(lo, q[0], q[1], ALU.subtract))
                    done(dve, tt(hi, q[2], q[3], ALU.add), rotated)
                for t in range(T):
                    dve.wait_ge(*proj(l, 8 + t + 1))
                    done(dve, nc.vector.tensor_copy(av[:, t, :], bank[t][:, :]), proj_dve)
                for t in range(T):
                    dve.wait_ge(*proj(l, 16 + t + 1))
                    done(dve, nc.vector.tensor_copy(bv[:, t, :], bank[t][:, 0:256]), proj_dve)
                if l == 0:
                    dve.wait_ge(*mh_stored(0, 1))
                for cc in range(1, 8, 2):
                    dve.wait_ge(*a_tr(l, cc + 1))
                    done(dve, nc.vector.tensor_copy(aT[:, cc, :], bank[cc][:, :]), aT_dve)
                dve.wait_ge(*ws_tr(l, 1))
                done(dve, tt(wsT[:, :, :], bank[3][:, :].rearrange("p (g t) -> p g t", g=G),
                             keep[:, None, :].broadcast_to([P, G, P])), ws_ready)
                group_sums(l, 0, sq_big.rearrange("p (n d) -> p n d", d=64), 16)
                group_scale(l, 0, cuv[:, :, 256:512].rearrange("p t (g d) -> p t g d", g=G), 16, 64, T, row("sgu"), cuv[:, :, 256:512])
                dve.wait_ge(*lam_exp(l, 1))
                lam_init = 0.8 - 0.6 * math.exp(-0.3 * l)
                step(tt(stat(LAM + 4), stat(LAM + 2), stat(LAM + 3), ALU.subtract))
                done(dve, scale_(stat(LAM + 5), stat(LAM + 4), -1.0, -lam_init), lam_ready)
                for j in range(2):
                    dve.wait_ge(*c_mm(l, j + 1))
                    mix4 = xn[:, 2 * j:2 * j + 2, 768:1024]
                    ps = bank[6 + j][:, :].rearrange("p (t g d) -> p t g d", t=2, g=G)
                    step(tt(mix4.rearrange("p t (g d) -> p t g d", g=G), ps,
                            bsp[:, None, :, None].broadcast_to([P, 2, G, 64]), ALU.add))
                    done(dve, tt(mix4, mix4, cuv[:, 2 * j:2 * j + 2, 0:256]), c_out)
                group_sums(l, 1, sq_big.rearrange("p (n d) -> p n d", d=64), 16)
                group_scale(l, 1, xn[:, :, 768:1024].rearrange("p t (g d) -> p t g d", g=G), 16, 64, T, row("c_out"), xn[:, :, 768:1024])

                def a_step(i):
                    if i < U:
                        n = P * (i // H + 1)
                        dve.wait_ge(*a_scores(l, i + 1))
                        for m in range(2):
                            step(nc.vector.reduce_max(stat(MAXA + 2 * i + m), bank[(2 * i + m) % 3][:, 0:n], AX.X))
                        done(dve, scale_(stat(MAXA + 2 * i, 2), stat(MAXA + 2 * i, 2), -0.125), a_max)
                    u = i - 1
                    if 0 <= u < U:
                        n = P * (u // H + 1)
                        p0, p1 = pa0[u % 3][:, 0:n], pa1[u % 2][:, 0:n]
                        dve.wait_ge(*a_exp(l, 2 * u + 2))
                        r = RLA + 2 * (u % 16)
                        step(nc.vector.reciprocal(stat(r, 2), stat(SUMA + 2 * u, 2)))
                        step(tt(stat(r + 1), stat(r + 1), stat(LAM + 5)))
                        step(scale_(p1, p1, stat(r + 1)))
                        done(dve, nc.vector.scalar_tensor_tensor(p0, p0, stat(r), p1, ALU.mult, ALU.add), a_comb)

                def a_norm(i):
                    if i >= 6 and (i - 6) % H == 0 and (i - 6) // H < T:
                        t = (i - 6) // H
                        dve.wait_ge(*a_pv(l, H * t + H))
                        done(dve, nc.vector.tensor_copy(xn[:, t, 0:512], bank[5][:, :]), a_out)
                    if i >= 7 and (i - 7) % H == 0 and (i - 7) // H < T:
                        group_sums(l, 2 + (i - 7) // H, sq.rearrange("p (h d) -> p h d", h=H), H)
                    if i >= 8 and (i - 8) % H == 0 and (i - 8) // H < T:
                        t = (i - 8) // H
                        group_scale(l, 2 + t, xn[:, t, 0:512].rearrange("p (h d) -> p h d", h=H), H, P, 0, row("subln"), None,
                                    1.0 - lam_init)

                def b_step(i):
                    h, part = i // 4, i % 4
                    if 1 <= h <= H and part == 0:
                        g = h - 1
                        dve.wait_ge(*b_pv(l, h))
                        done(dve, nc.vector.tensor_copy(xn[:, :, 512 + 64 * g:576 + 64 * g],
                                                        bank[3][:, 256:512].rearrange("p (t d) -> p t d", t=T)), b_out)
                    if h < H and part == 0:
                        for j, (a, n) in enumerate(B_JOB):
                            dve.wait_ge(*b_z(l, 3 * h + j + 1))
                            done(dve, scale_(sp_buf[:, a:a + n], bank[(6, 7, 3)[j]][:, 0:n], 17.0, None, ALU.min), b_min)
                    if h < H and part == 1:
                        for j, (a, n) in enumerate(B_JOB):
                            dve.wait_ge(*b_ln(l, 3 * h + j + 1))
                            step(tt(sp_buf[:, a:a + n], bank[(6, 7, 3)[j]][:, 0:n], sp_buf[:, a:a + n], ALU.max))
                        for kb in range(T):
                            d = sp_buf[:, B_AT[kb]:B_AT[kb] + P]
                            done(dve, tt(d, d, strict[:, :]), b_sp if kb == T - 1 else dve_step)
                    if h < H and part == 3:
                        dve.wait_ge(*b_w(l, 3 * h + 3))
                        for kb in range(T):
                            d = w_buf[:, B_AT[kb]:B_AT[kb] + P]
                            done(dve, tt(d, d, strict[:, :]), b_wm if kb == T - 1 else dve_step)

                for i in range(STEPS):
                    a_step(i)
                    b_step(i)
                    a_norm(i)
                group_sums(l, 6, cut(h_flat, 1280, 16, 64), 16)
                group_scale(l, 6, xn[:, :, 512:768].rearrange("p t (g d) -> p t g d", g=G), 16, 64, T, row("b_out"), xn[:, :, 512:768])

                for c in range(1, C, 2):
                    dve.wait_ge(*mix_tp(l, c + 1))
                    done(dve, nc.vector.tensor_copy(hT[:, c, :], bank[c][:, :]), mixT_dve)
                for j in range(8):
                    t, n = j % T, j // T
                    dve.wait_ge(*o_mm(l, j + 1))
                    xs = X[:, t, 512 * n:512 * n + 512]
                    done(dve, tt(xs, xs, bank[j][:, :], ALU.add), x_mix)

                norm(l, "cross")
                norm_evac(l, "cross", 1)
                for t in range(T):
                    dve.wait_ge(*c_scores(l, t + 1))
                    for j in range(2):
                        step(nc.vector.reduce_max(stat(MAXC + H * t + 2 * j, 2),
                                                  bank[2 + 2 * (t % 2) + j][:, :].rearrange("p (h m) -> p h m", h=2), AX.X))
                    done(dve, scale_(stat(MAXC + H * t, H), stat(MAXC + H * t, H), -0.125), c_max)
                    dve.wait_ge(*c_tp(l, 2 * t + 2))
                    if t >= 2:
                        dve.wait_ge(*c_pv(l, t - 1))
                    done(dve, nc.vector.tensor_copy(pcT[:, t % 2, 512:1024], bank[7][:, :]), c_pt_dve)
                    step(nc.vector.reciprocal(stat(RLC + H * t, H), stat(SUMC + H * t, H)))
                    dve.wait_ge(*c_pv(l, t + 1))
                    done(dve, tt(oc[:, t % 2, :].rearrange("p (h d) -> p h d", h=H),
                                 bank[t % 2][:, 0:256].rearrange("p (h d) -> p h d", h=H),
                                 stat(RLC + H * t, H)[:, :, None].broadcast_to([P, H, 64])), c_o)
                for j in range(8):
                    t, n = j // 2, j % 2
                    dve.wait_ge(*co_mm(l, j + 1))
                    xs = X[:, t, 512 * n:512 * n + 512]
                    done(dve, tt(xs, xs, bank[j][:, :], ALU.add), x_cross)

                norm(l, "ffn")
                norm_evac(l, "ffn", 2)

                lg = cut(rt, R_LOG, T, G + E)
                eg, e2 = cut(rt, R_EG, T, G), cut(rt, R_E2, T)
                og, el, o1, o2 = (cut(rt, a, T, G) for a in (R_OG, R_EL, R_O1, R_O2))
                tmp = cut(rt, R_TMP, T, G, G)
                pg, gi, i1 = cut(rt, R_PG, T), cut(rt, R_GI, T), cut(rt, R_I, T)
                prod, wide_ = cut(rt, R_PR, T, E), cut(rt, R_W, T, E)
                dve.wait_ge(*logits(l, 1))
                a, n = ROWS["route"]
                step(tt(lg, bank[0][:, 0:T * (G + E)].rearrange("p (t n) -> p t n", t=T),
                        rows[:, None, a:a + n].broadcast_to([P, T, G + E]), ALU.add))

                def over4(v):
                    return v[:, :, None].broadcast_to([P, T, 4])

                def first_max(vals, m, index, onehot):
                    step(nc.vector.tensor_reduce(m, vals, AX.X, ALU.max))
                    step(tt(onehot, vals, over4(m), ALU.is_ge))
                    step(scale_(onehot, onehot, -4.0, 4.0))
                    step(tt(onehot, onehot, iota4[:, None, :].broadcast_to([P, T, 4]), ALU.add))
                    step(nc.vector.tensor_reduce(index, onehot, AX.X, ALU.min))
                    step(tt(onehot, iota4[:, None, :].broadcast_to([P, T, 4]), over4(index), ALU.is_equal))

                gm, m1, m2 = stat(208, T), stat(212, T), stat(216, T)
                first_max(lg[:, :, 0:G], gm, gi, og)
                done(dve, tt(eg, lg[:, :, 0:G], over4(gm), ALU.subtract), r_max)
                step(tt(tmp, lg[:, :, G:].rearrange("p t (g j) -> p t g j", g=G),
                        og[:, :, :, None].broadcast_to([P, T, G, G])))
                step(nc.vector.tensor_reduce(el, tmp.rearrange("p t g j -> p t j g"), AX.X, ALU.add))
                first_max(el, m1, i1, o1)
                step(nc.vector.scalar_tensor_tensor(el, o1, NEG, el, ALU.mult, ALU.add))
                first_max(el, m2, i1, o2)
                done(dve, tt(e2, m2, m1, ALU.subtract), r_max)
                dve.wait_ge(*r_exp(l, 2))
                step(nc.vector.tensor_reduce(pg, eg, AX.X, ALU.add))
                step(nc.vector.reciprocal(pg, pg))
                g1, g2 = gate[:, 0, :], gate[:, 1, :]
                step(scale_(g2, e2, 1.0, None, ALU.add))
                step(nc.vector.reciprocal(g1, g2))
                step(tt(g1, g1, pg))
                step(tt(g2, g1, e2))
                for n, o in enumerate((o1, o2)):
                    step(tt(wide_[:, :, :].rearrange("p t (g j) -> p t g j", g=G), og[:, :, :, None].broadcast_to([P, T, G, G]),
                            o[:, :, None, :].broadcast_to([P, T, G, G])))
                    if n == 0:
                        step(nc.vector.tensor_copy(prod, wide_))
                done(dve, tt(mask_b[:, :, :], prod, wide_, ALU.add), masks)
                dve.wait_ge(*ranks(l, 1))
                rank = bank[1][:, 0:T * E].rearrange("p (t e) -> p t e", t=T)
                e16 = iotaE[:, None, :].broadcast_to([P, T, E])
                rs, es = stat(220, T), stat(224, T)
                buf = cut(rt, 384, T, E)
                for n, o in enumerate((prod, wide_)):
                    step(tt(buf, o, rank))
                    step(nc.vector.tensor_reduce(rs, buf, AX.X, ALU.add))
                    step(tt(buf, o, e16))
                    step(nc.vector.tensor_reduce(es, buf, AX.X, ALU.add))
                    step(nc.vector.scalar_tensor_tensor(pos_list.rearrange("p (t k) -> p k t", k=2)[:, n, :], rs, float(E), es, ALU.mult, ALU.add))
                    big, py = stat(232, T), stat(236, T)
                    step(scale_(big, rs, float(P), None, ALU.is_ge))
                    step(scale_(py, es, float(S - 2 * P), float(E * P - P)))
                    step(tt(big, big, py))
                    step(nc.vector.scalar_tensor_tensor(py, es, float(P), rs, ALU.mult, ALU.add))
                    step(tt(pos_y.rearrange("p (t k) -> p k t", k=2)[:, n, :], py, big, ALU.add))
                step(nc.vector.reduce_max(stat(228), bank[1][:, T * E:T * E + E], AX.X))
                done(dve, scale_(over[:, :], stat(228), float(P), None, ALU.is_gt), pos_ready)

                gain4 = gains[:, l, 2, :]

                def evac_rows(half, slot):
                    return tt(xgT[:, slot, 512 * half:512 * half + 512].rearrange("p (c s) -> p c s", c=4),
                              bank[6][:, :].rearrange("p (c s) -> p c s", c=4),
                              gain4[:, 4 * half:4 * half + 4][:, :, None].broadcast_to([P, 4, P]))

                def moe_step(k, a, gu=True, xt=True):
                    i = 2 * k + a
                    if xt:
                        for half in range(2):
                            dve.wait_ge(*xg_tp(l, 2 * (i + 1) + half + 1))
                            evac_rows(half, (a + 1) % 2).then_inc(xg_out.sem, 1)
                    if gu:
                        s, b = a % 2, 2 * (a % 2)
                        dve.wait_ge(*sig_exp(l, i + 1))
                        scale_(sg[:, s, :], sg[:, s, :], 1.0, None, ALU.add).then_inc(silu_step.sem, 1)
                        dve.wait_ge(*silu_step(l, 3 * i + 1))
                        nc.vector.reciprocal(sg[:, s, :], sg[:, s, :]).then_inc(silu_step.sem, 1)
                        dve.wait_ge(*silu_step(l, 3 * i + 2))
                        tt(sg[:, s, :], sg[:, s, :], bank[b][:, :]).then_inc(silu_step.sem, 1)
                        dve.wait_ge(*silu_step(l, 3 * i + 3))
                        if a >= 2:
                            dve.wait_ge(*act_tp(l, i - 1))
                        tt(act_[:, s, :], sg[:, s, :], bank[b + 1][:, :]).then_inc(act_ready.sem, 1)

                moe_step(0, -1, gu=False)
                moe_step(0, 0)
                moe_step(0, 1)
                moe_step(0, 2)
                with dve.Fori(0, 6) as k:
                    moe_step(k, 3)
                    moe_step(k, 4)
                moe_step(0, 15, xt=False)
                more = dve.value_load(over[0:1, 0:1], min_val=0, max_val=1)
                with dve.If(more > 0):
                    with dve.Fori(0, E) as e:
                        with dve.Fori(0, 3) as r:
                            n, od = 3 * e + r, over_dve[l].sem
                            for half in range(2):
                                dve.wait_ge(over_pe[l].sem, 5 * n + 1 + half + 1)
                                evac_rows(half, 0).then_inc(od, 1)
                            dve.wait_ge(over_act[l].sem, 4 * n + 1)
                            scale_(sg[:, 0, :], sg[:, 0, :], 1.0, None, ALU.add).then_inc(od, 1)
                            dve.wait_ge(od, 6 * n + 3)
                            nc.vector.reciprocal(sg[:, 0, :], sg[:, 0, :]).then_inc(od, 1)
                            dve.wait_ge(od, 6 * n + 4)
                            tt(sg[:, 0, :], sg[:, 0, :], bank[0][:, :]).then_inc(od, 1)
                            dve.wait_ge(od, 6 * n + 5)
                            tt(act_[:, 0, :], sg[:, 0, :], bank[1][:, :]).then_inc(od, 1)
                dve.end_ifs()
                for n in range(2 * T):
                    t, c = n // 2, n % 2
                    dve.wait_ge(*pair_loaded[n % 4](l, n // 4 + 1))
                    done(dve, nc.vector.scalar_tensor_tensor(X[:, t, :], yg[:, (n % 4) * D:(n % 4 + 1) * D], gate[:, c, t:t + 1],
                                                             X[:, t, :], ALU.mult, ALU.add), x_moe)

            norm(DEPTH, "mix")
            dve.wait_ge(*rows_loaded(DEPTH, 1))
            for t in range(T):
                done(dve, tt(X[:, t, :], xn[:, t, :], rows[:, 0:D]), out_ready)

        @block.tensor
        def _(pe):
            def mm(o, w, v, first=True, last=True):
                return nc.tensor.matmul(o, w, v, start=first, stop=last)

            def use(p, k=0):
                pe.wait_ge(piece_loaded[p % SLOTS].sem, 16 * (p // SLOTS + 1 + k))

            def wide(p, n):
                return piece(p)[:, 0:C * n].rearrange("p (c n) -> p c n", n=n)

            def norm_transpose(sig):
                for c in range(C):
                    for t in range(T):
                        ins = nc.tensor.transpose(bank[c][:, t * P:(t + 1) * P], xn[:, t, c::C], ident[:, :])
                    ins.then_inc(sig.sem, 1)

            pe.wait_ge(*consts_made(0, 11))
            pe.wait_ge(*mem_norm(0, MT))
            for j in range(4):
                for c in (2 * j, 2 * j + 1):
                    for t in range(MT):
                        ins = nc.tensor.transpose(bank[j][:, (c % 2) * M + t * P:(c % 2) * M + (t + 1) * P], mn[:, t, c::C], ident[:, :])
                ins.then_inc(mem_tp.sem, 1)

            for l in range(DEPTH):
                b = l * PIECES
                pe.wait_ge(*mg_ready(l, 1))
                if l == 0:
                    pe.wait_ge(*mh_done(0, 4))
                wk, wv = wide(b + K_V, 256), wide(b + K_V + 1, 256)
                for j in range(2):
                    if j == 0:
                        use(b + K_V)
                    for c in range(C):
                        ins = mm(bank[j][:, 0:M], wk[:, c, j * P:(j + 1) * P], mg[:, c, :], c == 0, c == C - 1)
                    ins.then_inc(kv.sem, 1)
                for t in range(MT):
                    if t == 0:
                        use(b + K_V + 1)
                    for c in range(C):
                        ins = mm(bank[2 + t][:, 0:256], mg[:, c, t * P:(t + 1) * P], wv[:, c, :], c == 0, c == C - 1)
                    ins.then_inc(kv.sem, 1)
                pe.wait_ge(*norm_xn["mix"](l, T))
                pe.wait_ge(*k_out(l, 2))
                pe.wait_ge(*v_out(l, 2))
                norm_transpose(norm_tp["mix"])
                pe.wait_ge(*norm_act["mix"](l, 4))
                pe.wait_ge(*norm_dve["mix"](l, 4))

                for j in range(24):
                    g, t = j // 4, j % 4
                    p = b + A_Q + g
                    n = 256 if g == 5 else 512
                    if t == 0:
                        use(p)
                    if 8 <= j < 16:
                        pe.wait_ge(*proj_act(l, j - 7))
                    elif 16 <= j < 20:
                        pe.wait_ge(*proj_dve(l, j - 15))
                    elif j >= 20:
                        pe.wait_ge(*proj_act(l, j - 11))
                    w = wide(p, n)
                    for c in range(C):
                        if g == 3:
                            ins = mm(bank[j % 8][:, :], w[:, c, t * P:(t + 1) * P], hT[:, c, :], c == 0, c == C - 1)
                        else:
                            ins = mm(bank[j % 8][:, 0:n], hT[:, c, t * P:(t + 1) * P], w[:, c, :], c == 0, c == C - 1)
                    ins.then_inc(proj.sem, 1)
                pe.wait_ge(*rotated(l, T))
                for cc in range(8):
                    pe.wait_ge(*proj_act(l, 12 + cc + 1))
                    for t in range(T):
                        ins = nc.tensor.transpose(bank[cc][:, t * P:(t + 1) * P], xn[:, t, cc * P:(cc + 1) * P], ident[:, :])
                    ins.then_inc(a_tr.sem, 1)
                pe.wait_ge(*wr_loaded(l, 3))
                pe.wait_ge(*aT_dve(l, 2))
                for g in range(G):
                    ins = nc.tensor.transpose(bank[3][:, g * P:(g + 1) * P], wsp[:, g, :], ident[:, :])
                ins.then_inc(ws_tr.sem, 1)
                pe.wait_ge(*ws_ready(l, 1))
                pe.wait_ge(*g_out(l, 1))
                pe.wait_ge(*aT_act(l, 4))
                pe.wait_ge(*aT_dve(l, 4))
                for t in range(T):
                    for g in range(G):
                        o = (t % 2) * 256 + g * 64
                        ins = mm(bank[6 + t // 2][:, o:o + 64], wsT[:, g, :], cuv[:, t, 256 + g * 64:320 + g * 64])
                    if t % 2:
                        ins.then_inc(c_mm.sem, 1)
                pe.wait_ge(*c_out(l, 2))
                if l == 0:
                    pe.wait_ge(*consts_made(0, 16))

                def a_step(i):
                    if i < U:
                        t, h = i // H, i % H
                        n = P * (t + 1)
                        for m in range(2):
                            job = 2 * i + m
                            if job >= 3:
                                pe.wait_ge(*a_exp(l, job - 2))
                            o, r = bank[job % 3], slice(64 * m, 64 * m + 64)
                            mm(o[:, 0:n], aT[r, h, t * P:(t + 1) * P], aT[r, 4 + h, 0:n], True, False)
                            ins = mm(o[:, t * P:n], ident_b[:, :], causal_b[:, :], False, True)
                        ins.then_inc(a_scores.sem, 1)
                    u = i - 2
                    if 0 <= u < U:
                        pe.wait_ge(*a_comb(l, u + 1))
                        if u:
                            pe.wait_ge(*a_pt(l, u))
                        for kb in range(u // H + 1):
                            ins = nc.tensor.transpose(bank[4][:, kb * P:(kb + 1) * P], pa0[u % 3][:, kb * P:(kb + 1) * P], ident[:, :])
                        ins.then_inc(a_tp.sem, 1)
                    u = i - 3
                    if 0 <= u < U:
                        t, h = u // H, u % H
                        pe.wait_ge(*a_pt(l, u + 1))
                        if h == 0 and t:
                            pe.wait_ge(*a_out(l, t))
                        for kb in range(t + 1):
                            ins = mm(bank[5][:, h * P:(h + 1) * P], pT[:, u % 2, kb * P:(kb + 1) * P], av[:, kb, h * P:(h + 1) * P],
                                     kb == 0, kb == t)
                        ins.then_inc(a_pv.sem, 1)

                def b_place(kb):
                    return ((6, 0), (7, 0), (3, 0), (7, 384))[kb]

                def b_step(i):
                    h, part = i // 4, i % 4
                    if h < H and part == 0:
                        if h:
                            pe.wait_ge(*b_w(l, 3 * h))
                            pe.wait_ge(*b_out(l, h))
                        r = slice(64 * (h % 2), 64 * (h % 2) + 64)
                        for kb in (0, 1, 3, 2):
                            bk, o = b_place(kb)
                            ins = nc.tensor.matmul(bank[bk][:, o:o + S - kb * P], bT[r, 2 + h // 2, kb * P:(kb + 1) * P],
                                                   bT[r, h // 2, kb * P:S], start=kb != 3, stop=False, skip_group_check=True)
                            if kb != 1:
                                ins.then_inc(b_z.sem, 1)
                    if h < H and part == 2:
                        pe.wait_ge(*b_sp(l, h + 1))
                        for kb in (0, 1, 3, 2):
                            bk, o = b_place(kb)
                            for k2 in range(kb, T):
                                n = S - k2 * P
                                ins = nc.tensor.matmul(bank[bk][:, o + (k2 - kb) * P:o + (k2 - kb) * P + n],
                                                       (neg_tri if k2 == kb else neg_one)[:, :], sp_buf[:, B_AT[k2]:B_AT[k2] + n],
                                                       start=False, stop=k2 == T - 1, skip_group_check=True)
                            if kb != 1:
                                ins.then_inc(b_sfx.sem, 1)
                    if h < H and part == 3:
                        pe.wait_ge(*b_wm(l, h + 1))
                        for t in range(T):
                            for kb in range(t + 1):
                                a = B_AT[kb] + (t - kb) * P
                                ins = mm(bank[3][:, 256 + t * 64:320 + t * 64], w_buf[:, a:a + P], bv[:, kb, h * 64:(h + 1) * 64],
                                         kb == 0, kb == t)
                        ins.then_inc(b_pv.sem, 1)

                pe.wait_ge(*lam_ready(l, 1))
                for i in range(STEPS):
                    a_step(i)
                    b_step(i)

                pe.wait_ge(*g_out(l, 7))
                for c in range(C):
                    for t in range(T):
                        ins = nc.tensor.transpose(bank[c][:, t * P:(t + 1) * P], xn[:, t, c::C], ident[:, :])
                    ins.then_inc(mix_tp.sem, 1)
                pe.wait_ge(*mixT_act(l, 4))
                pe.wait_ge(*mixT_dve(l, 4))
                for j in range(8):
                    t, n = j % T, j // T
                    if t == 0:
                        use(b + W_OUT + n)
                    w = wide(b + W_OUT + n, 512)
                    for c in range(C):
                        ins = mm(bank[j][:, :], hT[:, c, t * P:(t + 1) * P], w[:, c, :], c == 0, c == C - 1)
                    ins.then_inc(o_mm.sem, 1)

                pe.wait_ge(*x_mix(l, 8))
                pe.wait_ge(*norm_xn["cross"](l, T))
                norm_transpose(norm_tp["cross"])
                pe.wait_ge(*norm_act["cross"](l, 4))
                pe.wait_ge(*norm_dve["cross"](l, 4))
                use(b + W_CQ)
                w = wide(b + W_CQ, 256)
                for j in range(2):
                    for c in range(C):
                        ins = mm(bank[j][:, :], w[:, c, j * P:(j + 1) * P], hT[:, c, :], c == 0, c == C - 1)
                    ins.then_inc(cq.sem, 1)
                pe.wait_ge(*cq_out(l, 2))

                def scores(t):
                    for h in range(H):
                        r = slice(64 * (h % 2), 64 * (h % 2) + 64)
                        if h == 0 and t >= 2:
                            pe.wait_ge(*c_exp(l, t - 1))
                        ins = mm(bank[2 + 2 * (t % 2) + h % 2][:, (h // 2) * M:(h // 2 + 1) * M], cqT[r, h // 2, t * P:(t + 1) * P],
                                 kmT[r, h // 2, :])
                    ins.then_inc(c_scores.sem, 1)

                scores(0)
                for t in range(T):
                    if t + 1 < T:
                        scores(t + 1)
                    pe.wait_ge(*c_exp(l, t + 1))
                    if t:
                        pe.wait_ge(*c_pt_act(l, t))
                        pe.wait_ge(*c_pt_dve(l, t))
                    for h in range(H):
                        for kb in range(MT):
                            ins = nc.tensor.transpose(bank[6 + h // 2][:, ((h % 2) * 2 + kb) * P:((h % 2) * 2 + kb + 1) * P],
                                                      pc[:, t % 2, h, kb * P:(kb + 1) * P], ident[:, :])
                        if h % 2:
                            ins.then_inc(c_tp.sem, 1)
                    pe.wait_ge(*c_pt_act(l, t + 1))
                    pe.wait_ge(*c_pt_dve(l, t + 1))
                    if t >= 2:
                        pe.wait_ge(*c_ot(l, t - 1))
                    for h in range(H):
                        for kb in range(MT):
                            ins = mm(bank[t % 2][:, h * 64:(h + 1) * 64], pcT[:, t % 2, (2 * h + kb) * P:(2 * h + kb + 1) * P],
                                     vm[:, kb, h * 64:(h + 1) * 64], kb == 0, kb == MT - 1)
                    ins.then_inc(c_pv.sem, 1)
                    pe.wait_ge(*c_o(l, t + 1))
                    for c in range(2):
                        ins = nc.tensor.transpose(bank[t % 2][:, 256 + c * P:256 + (c + 1) * P], oc[:, t % 2, c::2], ident[:, :])
                    ins.then_inc(c_otp.sem, 1)
                pe.wait_ge(*c_ot(l, T))
                use(b + W_CO)
                wco = piece(b + W_CO)[:, 0:2 * D].rearrange("p (c n) -> p c n", c=2)
                for j in range(8):
                    t, n = j // 2, j % 2
                    for c in range(2):
                        ins = mm(bank[j][:, :], ocT[:, c, t * P:(t + 1) * P], wco[:, c, 512 * n:512 * n + 512], c == 0, c == 1)
                    ins.then_inc(co_mm.sem, 1)

                pe.wait_ge(*x_cross(l, 8))
                pe.wait_ge(*norm_xn["ffn"](l, T))
                norm_transpose(norm_tp["ffn"])
                pe.wait_ge(*norm_act["ffn"](l, 4))
                pe.wait_ge(*norm_dve["ffn"](l, 4))
                for t in range(T):
                    for c in range(C):
                        ins = mm(bank[0][:, t * 20:t * 20 + 20], hT[:, c, t * P:(t + 1) * P], wr[:, c, :], c == 0, c == C - 1)
                ins.then_inc(logits.sem, 1)
                pe.wait_ge(*masks(l, 1))
                for t in range(T):
                    for t2 in range(t + 1):
                        mm(bank[1][:, t * E:(t + 1) * E], (strict_b if t2 == t else one_b)[:, :], mask_b[:, t2, :], t2 == 0, t2 == t)
                for t in range(T):
                    ins = mm(bank[1][:, T * E:T * E + E], one_b[:, :], mask_b[:, t, :], t == 0, t == T - 1)
                ins.then_inc(ranks.sem, 1)
                pe.wait_ge(*pos_ready(l, 1))

                def rows_half(slot, half):
                    for q in range(4):
                        ins = nc.tensor.transpose(bank[6][:, q * P:(q + 1) * P], xg[:, slot, 4 * half + q::C], ident[:, :])
                    return ins

                def product(o, stationary, w, chunks):
                    for c in range(chunks):
                        ins = mm(o, stationary[:, c * P:(c + 1) * P], w[:, c, :], c == 0, c == chunks - 1)
                    return ins

                def moe_step(k, a, gu=True, xt=True, dn=True):
                    i = 2 * k + a
                    p = b + W_EXP + 3 * a - 1 + (1 if a == 0 else 0)
                    s, bk = a % 2, 2 * (a % 2)
                    if gu:
                        use(p, k)
                        pe.wait_ge(*xg_out(l, 2 * i + 2))
                        if a >= 2:
                            pe.wait_ge(*act_ready(l, i - 1))
                        product(bank[bk][:, :], xgT[:, s, :], wide(p, 512), C).then_inc(gate_done.sem, 1)
                    if dn:
                        pe.wait_ge(*act_ready(l, i))
                        if a >= 2:
                            pe.wait_ge(*actT_out(l, i - 1))
                        for q in range(FC):
                            ins = nc.tensor.transpose(bank[7][:, q * P:(q + 1) * P], act_[:, (a - 1) % 2, q::FC], ident[:, :])
                        ins.then_inc(act_tp.sem, 1)
                    if xt:
                        pe.wait_ge(*gathered[(a + 1) % 2](l, k + (a + 1) // 2 + 1))
                        if a >= 0:
                            pe.wait_ge(*xg_out(l, 2 * i + 2))
                        rows_half((a + 1) % 2, 0).then_inc(xg_tp.sem, 1)
                    if gu:
                        use(p + 1, k)
                        product(bank[bk + 1][:, :], xgT[:, s, :], wide(p + 1, 512), C).then_inc(gate_up.sem, 1)
                    if xt:
                        pe.wait_ge(*xg_out(l, 2 * i + 3))
                        rows_half((a + 1) % 2, 1).then_inc(xg_tp.sem, 1)
                    if dn:
                        q = p + 2 if gu else b + PIECES - 1
                        use(q, k)
                        pe.wait_ge(*actT_out(l, i))
                        if a >= 2:
                            pe.wait_ge(*y_out(l, 2 * i - 2))
                        w = piece(q).rearrange("p (c n) -> p c n", c=FC)
                        for n in range(2):
                            ins = product(bank[4 + n][:, :], actT[:, (a - 1) % 2, :], w[:, :, 512 * n:512 * n + 512], FC)
                            ins.then_inc(down.sem, 1)

                moe_step(0, -1, gu=False, dn=False)
                moe_step(0, 0, dn=False)
                moe_step(0, 1)
                moe_step(0, 2)
                with pe.Fori(0, 6) as k:
                    moe_step(k, 3)
                    moe_step(k, 4)
                moe_step(0, 15, xt=False)
                moe_step(0, 16, gu=False, xt=False)
                more = pe.value_load(over[0:1, 0:1], min_val=0, max_val=1)
                with pe.If(more > 0):
                    op = over_pe[l].sem
                    pe.wait_ge(*y_out(l, 2 * E))
                    pe.sem_inc(op, 1)
                    with pe.Fori(0, E) as e:
                        with pe.Fori(0, 3) as r:
                            n = 3 * e + r
                            pe.wait_ge(over_x[l].sem, 16 * n + 16)
                            rows_half(0, 0).then_inc(op, 1)
                            pe.wait_ge(over_dve[l].sem, 6 * n + 1)
                            rows_half(0, 1).then_inc(op, 1)
                            pe.wait_ge(over_dve[l].sem, 6 * n + 2)
                            pe.wait_ge(over_w[l].sem, 48 * n + 48)
                            product(bank[0][:, :], xgT[:, 0, :], wide(0, 512), C)
                            product(bank[1][:, :], xgT[:, 0, :], wide(1, 512), C).then_inc(op, 1)
                            pe.wait_ge(over_dve[l].sem, 6 * n + 6)
                            for q in range(FC):
                                ins = nc.tensor.transpose(bank[7][:, q * P:(q + 1) * P], act_[:, 0, q::FC], ident[:, :])
                            ins.then_inc(op, 1)
                            pe.wait_ge(over_act[l].sem, 4 * n + 2)
                            w = piece(2).rearrange("p (c n) -> p c n", c=FC)
                            for q in range(2):
                                ins = product(bank[4 + q][:, :], actT[:, 0, :], w[:, :, 512 * q:512 * q + 512], FC)
                            ins.then_inc(op, 1)
                            pe.wait_ge(over_y[l].sem, 16 * n + 16)
                pe.end_ifs()


NAMES = ["x", "mem", "positions", "norm_mix", "w_in", "lam_q1", "lam_k1", "lam_q2", "lam_k2", "subln_a",
         "norm_b_out", "sgu_norm", "w_spatial", "b_spatial", "norm_c_out", "w_out", "norm_cross", "norm_mem",
         "w_cq", "w_ck", "w_cv", "w_co", "norm_ffn", "w_group", "b_group", "w_router", "b_router",
         "w_gate", "w_up", "w_down", "norm_final"]


def kernel(**inputs):
    import concourse.bacc as bacc
    from concourse.bass_utils import run_bass_kernel_spmd

    nc = bacc.Bacc("TRN2", target_bir_lowering=False, num_devices=1)
    arrays, args = {}, []
    for name in NAMES:
        a = np.ascontiguousarray(inputs[name])
        arrays[f"in_{name}"] = a
        args.append(nc.dram_tensor(f"in_{name}", a.shape, mybir.dt.from_np(a.dtype), kind="ExternalInput").ap())
    args.append(nc.dram_tensor("out", (1, S, D), F32, kind="ExternalOutput").ap())
    trunk(nc, *args)
    return run_bass_kernel_spmd(nc, [arrays], core_ids=[0]).results[0]["out"]
```

```python
import math
from contextlib import ExitStack

import numpy as np

import concourse.bass as bass
from concourse import mybir

F32, F32R, BF16, I32 = mybir.dt.float32, mybir.dt.float32r, mybir.dt.bfloat16, mybir.dt.int32
ALU, ACT, AX = mybir.AluOpType, mybir.ActivationFunctionType, mybir.AxisListType

P = 128
D, S, DEPTH, M = 1024, 512, 2, 256
T, C, MT = S // P, D // P, M // P
H = 4
E, G, F = 16, 4, 512
FC = F // P
EPS = 1e-6
NEG = -1e30
ROPE_THETA, ROPE_DIM = 500000.0, 16
HALF = ROPE_DIM // 2
SLOTS = 6
PW = C * 512
WORK = 11264
W_OUT, W_CQ, W_CO, W_NEXT = 6, 8, 9, 10


def first_piece(l):
    return 2 + l * (12 + 3 * E)


def memory_piece(l):
    return first_piece(l - 1) + W_NEXT if l else 0


def expert_piece(l):
    return first_piece(l) + (12 if l + 1 < DEPTH else 10)


ORDER = (4, 5, 0, 1, 2, 3)
PIECES = expert_piece(DEPTH - 1) + 3 * E
SPLIT_SLOTS = (4, 5)


def slot(p):
    if p < 2:
        return (2, 3)[p]
    l = 0 if p < first_piece(1) else 1
    if p >= expert_piece(l):
        return (p - expert_piece(l) + 4) % SLOTS
    return (p - first_piece(l)) % 4


TURN = [sum(slot(q) == slot(p) for q in range(p)) for p in range(PIECES)]
STEPS = T * H + 4
OVER = 3 * E

B_AT = [0, 512, 1024, 896]
B_JOB = [(0, 512), (512, 512), (1024, 256)]
ROWS = {"subln": (0, 128), "b_out": (128, 256), "sgu": (384, 256), "c_out": (640, 256),
        "lam": (896, 256), "route": (1152, G + E)}


class Signal:

    def __init__(self, sem, per_layer=0, unit=1):
        self.sem, self.per_layer, self.unit, self.count = sem, per_layer, unit, 0

    def __call__(self, l, k):
        return self.sem, (k + l * self.per_layer) * self.unit


def done(engine, ins, sig):
    ins.then_inc(sig.sem, 1)
    sig.count += 1
    engine.wait_ge(sig.sem, sig.count)


def trunk(nc, x, mem, positions, norm_mix, w_in, lam_q1, lam_k1, lam_q2, lam_k2, subln_a,
          norm_b_out, sgu_norm, w_spatial, b_spatial, norm_c_out, w_out, norm_cross, norm_mem,
          w_cq, w_ck, w_cv, w_co, norm_ffn, w_group, b_group, w_router, b_router,
          w_gate, w_up, w_down, norm_final, out):
    ctx = ExitStack()
    with ctx:
        def sb(name, shape, dt=F32):
            return ctx.enter_context(nc.sbuf_tensor(name, shape, dt))

        def sem(name):
            return ctx.enter_context(nc.semaphore(name))

        with nc.sbuf_tensor("ring_r", [P, SLOTS, PW], F32R) as ring_r:
            pass
        ring = sb("ring", [P, SLOTS, PW])
        X = sb("X", [P, T, D])
        with nc.sbuf_tensor("split_r", [P, C * S + WORK + T * D], F32R) as split_r:
            pass
        hT = sb("hT", [P, C, S])
        work = sb("work", [P, WORK])
        xn = sb("xn", [P, T, D])
        kmT = sb("kmT", [P, 2, M])
        vm = sb("vm", [P, MT, 256])
        wsT = sb("wsT", [P, G, P])
        rows = sb("rows", [P, 1172])
        gains = sb("gains", [P, DEPTH, 4, C])
        wr = sb("wr", [P, C, G + E])
        bsp = sb("bsp", [P, G])
        ident = sb("ident", [P, P])
        ident_b = sb("ident_b", [P, P], BF16)
        causal_b = sb("causal_b", [P, P], BF16)
        strict = sb("strict", [P, P])
        strict_b = sb("strict_b", [P, P], BF16)
        keep = sb("keep", [P, P])
        neg_tri = sb("neg_tri", [P, P])
        neg_one = sb("neg_one", [P, P])
        one_b = sb("one_b", [P, P], BF16)
        st = sb("st", [P, 256])
        cs = sb("cs", [P, 2, T, HALF])
        rt = sb("rt", [P, 512])
        mask_b = sb("mask_b", [P, T, E], BF16)
        iota4 = sb("iota4", [P, 4])
        iotaE = sb("iotaE", [P, E])
        slot_b = sb("slot_b", [P, P], BF16)
        lane = sb("lane", [P, 1])
        tile_base = sb("tile_base", [P, T, E])
        zero_i = sb("zero_i", [P, E], I32)
        tok_id = sb("tok_id", [P, T], I32)
        pos_list = sb("pos_list", [P, 2 * T], I32)
        pos_y = sb("pos_y", [P, 2 * T], I32)
        gate = sb("gate", [P, 2, T])
        lists = sb("lists", [P, E], I32)
        over = sb("over", [P, 1], I32)
        over_ids = sb("over_ids", [P, 1], I32)
        pos_i = sb("pos_i", [P, T], I32)
        eps_col = sb("eps_col", [P, 1])
        bank = [ctx.enter_context(nc.psum_tensor(f"bank{i}", [P, 512], F32)) for i in range(8)]

        xn_dram = nc.dram_tensor("xn_dram", [S, D], F32).ap()
        y_dram = nc.dram_tensor("y_dram", [E * S, D], F32).ap()
        list_dram = nc.dram_tensor("list_dram", [S * E, 1], I32).ap()
        mh_dram = nc.dram_tensor("mh_dram", [P, C * M], F32).ap()

        def cut(buf, start, *shape):
            n = int(np.prod(shape))
            v = buf[:, start:start + n]
            if len(shape) == 2:
                return v.rearrange("p (a b) -> p a b", a=shape[0])
            if len(shape) == 3:
                return v.rearrange("p (a b c) -> p a b c", a=shape[0], b=shape[1])
            return v

        hT_r = split_r[:, 0:2 * C * S].rearrange("p (w c s) -> p w c s", w=2, c=C)
        down_r = (split_r[:, 0:PW], split_r[:, C * S + WORK:C * S + WORK + PW])
        actT_r = split_r[:, C * S + 9216:C * S + 11264].rearrange("p (s w n) -> p s w n", s=2, w=2)

        aT = cut(work, 0, 8, S)
        bT = cut(work, 4096, 4, S)
        av = cut(work, 6144, T, 512)
        bv = cut(work, 8192, T, 256)
        rot = cut(work, 4096, 4, 128)
        sq_c = cut(work, 4608, 1024)
        cuv = cut(work, 9216, T, 512)
        mhT = cut(work, 0, C, M)
        mg = cut(work, 9216, C, M)
        mraw = cut(work, 9216, MT, D)
        mn = cut(work, 4096, MT, D)
        pa0 = [cut(work, 9216, 512), cut(work, 10240, 512), rt[:, 0:512]]
        pa1 = [cut(work, 9728, 512), cut(work, 10752, 512)]
        h_flat = hT[:, :, :].rearrange("p c s -> p (c s)")
        sp_buf = h_flat[:, 0:1280]
        w_buf = h_flat[:, 1280:2560]
        pT = cut(h_flat, 2560, 2, 512)
        sq = h_flat[:, 3584:4096]
        cqT = cut(work, 0, 2, S)
        pc = cut(work, 1024, 2, H, M)
        pcT = cut(work, 3072, 2, 1024)
        oc = cut(work, 5120, 2, 256)
        ocT = cut(work, 5632, 2, S)
        xg = cut(work, 0, 2, D)
        xgT = cut(work, 2048, 2, D)
        sg = cut(work, 4096, 2, F)
        act_ = cut(work, 5120, 2, F)
        actT = cut(work, 6144, 2, F)
        yo = cut(work, 7168, 2, D)
        yg = cut(work, 3072, 2 * T, D)
        hot = h_flat[:, 0:512].bitcast(BF16).rearrange("p (k t s) -> p k t s", k=2, t=T)
        ids_b = h_flat[:, 512:640].bitcast(BF16).rearrange("p (k w t e) -> p k w t e", k=2, w=2, t=T)
        wsp = cut(rt, 0, G, P)

        def piece(p):
            return ring[:, slot(p), :]

        def piece_half(p, half, n):
            return piece(p)[:, half * 4 * n:(half + 1) * 4 * n].rearrange("p (c n) -> p c n", n=n)

        def split_half(half, n):
            buf = ring_r[:, SPLIT_SLOTS[half], :]
            return [buf[:, a:a + 4 * n].rearrange("p (c n) -> p c n", n=n) for a in (0, PW // 2)]

        def stat(i, n=1):
            return st[:, i:i + n]

        R_LOG, R_EG, R_E2, R_OG, R_PG, R_EL, R_TMP, R_O1, R_O2, R_GI, R_I, R_PR, R_W = (
            0, 80, 96, 104, 120, 128, 144, 208, 224, 240, 244, 252, 316)
        SS, SEED, TMP = 0, 16, 32
        MAXA, SUMA = 48, 80
        RLA = 112
        MAXC, SUMC, RLC = 144, 160, 176
        LAM = 192


        def signal(name, per_layer=0, unit=1):
            return Signal(sem(name), per_layer, unit)

        consts_made, eps_made, mh_done = signal("consts_made"), signal("eps_made"), signal("mh_done")
        wr_loaded = [signal(f"wr_loaded_{l}", unit=16) for l in range(DEPTH)]
        x_loaded, mem_loaded = signal("x_loaded", unit=16), signal("mem_loaded", unit=16)
        list_written = [signal(f"list_written_{l}", unit=16) for l in range(DEPTH)]
        piece_loaded = [signal(f"piece_loaded_{i}", 0, 16) for i in range(SLOTS)]
        act_step, dve_step, pool_step = signal("act_step"), signal("dve_step"), signal("pool_step")
        angles, rope = signal("angles"), signal("rope")
        mem_seed, mem_norm, mem_tp = signal("mem_seed"), signal("mem_norm"), signal("mem_tp")
        mh_stored, mh_loaded = signal("mh_stored", 0, 16), signal("mh_loaded", 1, 16)
        rows_loaded = [signal(f"rows_loaded_{l}", unit=16) for l in range(DEPTH + 1)]
        gains_loaded = signal("gains_loaded", 0, 16)
        norm_seed = {n: signal(f"norm_{n}_seed", T) for n in ("mix", "cross", "ffn")}
        norm_xn = {n: signal(f"norm_{n}_xn", T) for n in norm_seed}
        norm_tp = {n: signal(f"norm_{n}_tp", 2 * T) for n in norm_seed}
        norm_act = {n: signal(f"norm_{n}_act", C * T if n == "mix" else T) for n in norm_seed}
        norm_dve = {n: signal(f"norm_{n}_dve", T) for n in norm_seed}
        mg_ready, kv, k_out, v_out = signal("mg_ready", 1), signal("kv", 4), signal("k_out", 2), signal("v_out", 2)
        w_hi, half_used = signal("w_hi", 16), signal("half_used", 8)
        w_lo_dve, w_lo_pool = signal("w_lo_dve", 14), signal("w_lo_pool", 2)
        proj, proj_act, proj_dve = signal("proj", 24), signal("proj_act", 20), signal("proj_dve", 8)
        rotated, a_tr, aT_act, aT_dve = signal("rotated", T), signal("a_tr", 8), signal("aT_act", 4), signal("aT_dve", 4)
        ws_tr, ws_ready, c_mm, c_out = signal("ws_tr", 1), signal("ws_ready", 1), signal("c_mm", 2), signal("c_out", 2)
        g_sq, g_ss, g_seed, g_out = (signal(n, k) for n, k in (("g_sq", 6), ("g_ss", 6), ("g_seed", 7), ("g_out", 7)))
        lam_sum, lam_exp, lam_ready = signal("lam_sum", 1), signal("lam_exp", 1), signal("lam_ready", 1)
        U = T * H
        a_scores, a_max, a_exp, a_comb = signal("a_scores", 2 * U), signal("a_max", 2 * U), signal("a_exp", 2 * U), signal("a_comb", U)
        a_tp, a_pt, a_pv, a_out = signal("a_tp", U), signal("a_pt", U), signal("a_pv", U), signal("a_out", T - 1)
        b_max = signal("b_max", H)
        b_z, b_min, b_ln, b_sp = signal("b_z", 3 * H), signal("b_min", 3 * H), signal("b_ln", 3 * H), signal("b_sp", H)
        b_sfx, b_w, b_wm, b_pv, b_out = signal("b_sfx", 3 * H), signal("b_w", 3 * H), signal("b_wm", H + 1), signal("b_pv", H), signal("b_out", H)
        mix_tp, mixT_hi, mixT_lo = signal("mix_tp", C), signal("mixT_hi", C), signal("mixT_lo", C)
        o_mm, x_mix = signal("o_mm", 8), signal("x_mix", 8)
        cq, cq_out = signal("cq", 2), signal("cq_out", 2)
        c_scores, c_max, c_exp = signal("c_scores", T), signal("c_max", T), signal("c_exp", T)
        c_tp, c_pt_act, c_pt_dve, c_pv, c_o = signal("c_tp", 2 * T), signal("c_pt_act", T), signal("c_pt_dve", T), signal("c_pv", T), signal("c_o", T)
        c_otp, c_ot, co_mm, x_cross = signal("c_otp", T), signal("c_ot", T), signal("co_mm", 8), signal("x_cross", 8)
        xn_stored, logits, r_max, r_exp, masks = signal("xn_stored", 1, 16), signal("logits", 1), signal("r_max", 2), signal("r_exp", 2), signal("masks", 1)
        ranks, pos_ready, lists_ready = signal("ranks", 1), signal("pos_ready", 1), signal("lists_ready", 1)
        gathered = [signal(f"gathered_{i}", E // 2, 16) for i in range(2)]
        xg_tp, xg_out, gate_up, silu_done, act_ready = signal("xg_tp", 2 * E), signal("xg_out", 2 * E), signal("gate_up", E), signal("silu_done", E), signal("act_ready", E)
        gate_done = signal("gate_done", E)
        hot_ready, lists_mm = signal("hot_ready", 1), signal("lists_mm", 1)
        d_hi, d_lo, actT_lo = signal("d_hi", 2 * E - 2), signal("d_lo", 2 * E - 2), signal("actT_lo", E - 1)
        act_tp, actT_out, down, y_out = signal("act_tp", E), signal("actT_out", E), signal("down", 2 * E), signal("y_out", 2 * E)
        y_stored = [signal(f"y_stored_{i}", E // 2, 16) for i in range(2)]
        over_w = [signal(f"over_w_{l}", unit=16) for l in range(DEPTH)]
        over_ids_in = [signal(f"over_ids_in_{l}", unit=16) for l in range(DEPTH)]
        over_go = [signal(f"over_go_{l}") for l in range(DEPTH)]
        over_x = [signal(f"over_x_{l}", unit=16) for l in range(DEPTH)]
        over_y = [signal(f"over_y_{l}", unit=16) for l in range(DEPTH)]
        over_pe = [signal(f"over_pe_{l}") for l in range(DEPTH)]
        over_act = [signal(f"over_act_{l}") for l in range(DEPTH)]
        over_dve = [signal(f"over_dve_{l}") for l in range(DEPTH)]
        pair_loaded = [signal(f"pair_loaded_{i}", 2, 16) for i in range(T)]
        x_moe, out_ready, out_stored = signal("x_moe", 2 * T), signal("out_ready"), signal("out_stored", unit=16)

        y_first = y_dram[0:E * P, :].rearrange("(e s) d -> e s d", e=E)
        y_over = y_dram[E * P:E * S, :].rearrange("(e r s) d -> e r s d", e=E, r=3)

        block = ctx.enter_context(nc.Block())

        def load_rows(eng, l):
            for n, v in enumerate((lam_q1, lam_q2, lam_k1, lam_k2)):
                a = ROWS["lam"][0] + 64 * n
                eng.dma_start(rows[:, a:a + 64], v[l].partition_broadcast(P)).then_inc(rows_loaded[l].sem, 16)
            for name, v in (("subln", subln_a), ("b_out", norm_b_out), ("sgu", sgu_norm), ("c_out", norm_c_out)):
                a, n = ROWS[name]
                eng.dma_start(rows[:, a:a + n], v[l].partition_broadcast(P)).then_inc(rows_loaded[l].sem, 16)
            a = ROWS["route"][0]
            eng.dma_start(rows[:, a:a + G], b_group[l].partition_broadcast(P)).then_inc(rows_loaded[l].sem, 16)
            eng.dma_start(rows[:, a + G:a + G + E], b_router[l].partition_broadcast(P)).then_inc(rows_loaded[l].sem, 16)
            eng.dma_start(bsp[:, :], b_spatial[l].rearrange("g t -> t g"),
                          allow_slow_non_contiguous=True).then_inc(rows_loaded[l].sem, 16)
            eng.dma_start(wr[:, :, 0:G], w_group[l].rearrange("(p c) g -> p c g", c=C)).then_inc(wr_loaded[l].sem, 16)
            eng.dma_start(wr[:, :, G:G + E], w_router[l].rearrange("(p c) g -> p c g", c=C)).then_inc(wr_loaded[l].sem, 16)
            eng.dma_start(wsp[:, :, :], w_spatial[l].rearrange("g t s -> t g s")).then_inc(wr_loaded[l].sem, 16)

        def split_piece(l, q):
            return first_piece(l) + q // 2, q % 2, 256 if q // 2 == 1 else 512

        def w_lo(l, q):
            return w_lo_pool(l, q - 11) if q in (12, 13) else w_lo_dve(l, q + 1 if q < 12 else q - 1)

        def wait_piece(eng, p, k=0):
            eng.wait_ge(piece_loaded[slot(p)].sem, 16 * (TURN[p] + 1 + k))

        def down_piece(l, a):
            return expert_piece(l) + (3 * a + 1 if a < E else 3 * E - 1)

        def wait_split_free(eng, l, q):
            if q % 2 == 0 and q >= 2:
                eng.wait_ge(*half_used(l, q // 2))
            elif q == 15:
                eng.wait_ge(*o_mm(l, 4))
            elif q >= 3:
                eng.wait_ge(*proj(l, 2 * (q - 1)))

        @block.sync
        def _(sp):
            released = [None] * PIECES
            for l in range(DEPTH):
                m, f, x_ = memory_piece(l), first_piece(l), expert_piece(l)
                released[m:m + 2] = [kv(l, 2), kv(l, 4)]
                released[f:f + 10] = [w_lo(l, 2 * n + 1) for n in range(8)] + [cq(l, 2), co_mm(l, 8)]
                released[x_:x_ + 2] = [gate_done(l, 1), gate_up(l, 1)]
                for i in range(1, E):
                    released[x_ + 3 * i - 1:x_ + 3 * i + 2] = [gate_done(l, i + 1), gate_up(l, i + 1), d_lo(l, 2 * i)]
                released[x_ + 3 * E - 1] = down(l, 2 * E)

            def load(p, dst, src, wait=True):
                if TURN[p] and wait:
                    sp.wait_ge(*released[max(q for q in range(p) if slot(q) == slot(p))])
                sp.dma_start(dst, src).then_inc(piece_loaded[slot(p)].sem, 16)

            def wide(p, n):
                return piece(p)[:, 0:C * n].rearrange("p (c n) -> p c n", n=n)

            def columns(w, a, n):
                return w[:, a:a + n].rearrange("(p c) n -> p c n", c=C)

            def memory_weights(l):
                for n, w in enumerate((w_ck, w_cv)):
                    p = memory_piece(l) + n
                    load(p, wide(p, 256), columns(w[l], 0, 256))

            for t in range(T):
                sp.dma_start(X[:, t, :], x[0, t * P:(t + 1) * P, :]).then_inc(x_loaded.sem, 16)
            for l in range(DEPTH):
                f, b = first_piece(l), expert_piece(l)
                if l == 0:
                    memory_weights(0)
                for n, g in enumerate(ORDER):
                    if l and n == 3:
                        sp.wait_ge(*pair_loaded[T - 1](l - 1, 2))
                    load(f + n, wide(f + n, 512 if g < 5 else 256), columns(w_in[l], 512 * g, 512 if g < 5 else 256))
                for n in range(2):
                    load(f + W_OUT + n, wide(f + W_OUT + n, 512), columns(w_out[l], 512 * n, 512))
                load(f + W_CQ, wide(f + W_CQ, 256), columns(w_cq[l], 0, 256))
                load(f + W_CO, piece(f + W_CO)[:, 0:2 * D], w_co[l].rearrange("(p c) n -> p (c n)", c=2))
                if l + 1 < DEPTH:
                    memory_weights(l + 1)
                sp.wait_ge(*o_mm(l, 8))
                gate_v = w_gate[l].rearrange("e (p c) f -> e p (c f)", c=C)
                up_v = w_up[l].rearrange("e (p c) f -> e p (c f)", c=C)
                down_v = w_down[l].rearrange("e (p c) n -> e p (c n)", c=FC)

                def expert(i):
                    p = b + (3 * i - 1 if i else 0)
                    load(p, piece(p), gate_v[i])
                    load(p + 1, piece(p + 1), up_v[i])
                    if i:
                        load(p + 2, piece(p + 2), down_v[i - 1])

                def expert_in_loop(k, a):
                    i, p = 2 * k + a, b + 3 * a - 1
                    sp.wait_ge(*gate_done(l, i - 1))
                    load(p, piece(p), gate_v[i], False)
                    sp.wait_ge(*gate_up(l, i - 1))
                    load(p + 1, piece(p + 1), up_v[i], False)
                    sp.wait_ge(*d_lo(l, 2 * i - 4))
                    load(p + 2, piece(p + 2), down_v[i - 1], False)

                for i in range(3):
                    expert(i)
                with sp.Fori(0, 6) as k:
                    expert_in_loop(k, 3)
                    expert_in_loop(k, 4)
                expert(15)
                p = b + 3 * E - 1
                load(p, piece(p), down_v[E - 1])
                sp.wait_ge(*pos_ready(l, 1))
                more = sp.value_load(over[0:1, 0:1], min_val=0, max_val=1)
                with sp.If(more > 0):
                    sp.wait_ge(*down(l, 2 * E))
                    with sp.Fori(0, E) as e:
                        with sp.Fori(0, 3) as r:
                            sp.wait_ge(over_pe[l].sem, e * 15 + r * 5 + 1)
                            for n, w in enumerate((gate_v, up_v, down_v)):
                                sp.dma_start(ring[:, n, :], w[e]).then_inc(over_w[l].sem, 16)
                    sp.wait_ge(*over_w[l](0, 3 * OVER))
                    sp.wait_ge(*over_pe[l](0, 5 * OVER + 1))
                sp.end_ifs()

        @block.gpsimd
        def _(pool):
            def const(ins):
                done(pool, ins, consts_made)

            for m, v in ((ident, 0.0), (ident_b, 0.0), (causal_b, 0.0), (strict, 1.0), (strict_b, 1.0),
                         (keep, 1.0), (neg_tri, -1.0), (neg_one, -1.0), (one_b, 1.0)):
                const(nc.gpsimd.memset(m[:, :], v))

            def select(m, op, fill, base, cm, step):
                const(nc.gpsimd.affine_select(out=m[:, :], in_=m[:, :], compare_op=op, fill=fill, base=base,
                                              pattern=[[step, P]], channel_multiplier=cm))

            select(ident, ALU.not_equal, 1.0, 0, 1, -1)
            select(ident_b, ALU.not_equal, 1.0, 0, 1, -1)
            select(causal_b, ALU.is_ge, NEG, 0, 1, -1)
            select(strict, ALU.is_gt, 0.0, 0, -1, 1)
            select(strict_b, ALU.is_gt, 0.0, 0, -1, 1)
            select(keep, ALU.is_ge, 0.0, 0, -1, 1)
            select(neg_tri, ALU.is_ge, 0.0, 0, 1, -1)
            const(nc.gpsimd.iota(tok_id[:, :], pattern=[[P, T]], base=0, channel_multiplier=1))
            const(nc.gpsimd.iota(iota4[:, :], pattern=[[1, 4]], base=0, channel_multiplier=0,
                                 allow_small_or_imprecise_dtypes=True))
            const(nc.gpsimd.iota(iotaE[:, :], pattern=[[1, E]], base=0, channel_multiplier=0,
                                 allow_small_or_imprecise_dtypes=True))
            const(nc.gpsimd.iota(slot_b[:, :], pattern=[[1, P]], base=0, channel_multiplier=0,
                                 allow_small_or_imprecise_dtypes=True))
            const(nc.gpsimd.iota(lane[:, :], pattern=[[1, 1]], base=0, channel_multiplier=1,
                                 allow_small_or_imprecise_dtypes=True))
            const(nc.gpsimd.iota(tile_base[:, :, :], pattern=[[P, T], [0, E]], base=0, channel_multiplier=0,
                                 allow_small_or_imprecise_dtypes=True))
            const(nc.gpsimd.memset(zero_i[:, :], 0))

            def combine(l, y):
                pool.wait_ge(*y_stored[0](l, E // 2))
                pool.wait_ge(*y_stored[1](l, E // 2))
                for n in range(2 * T):
                    pool.indirect_dma_start(out=yg[:, n, :], out_offset=None, in_=y,
                                            in_offset=bass.IndirectOffsetOnAxis(ap=pos_y[:, n:n + 1], axis=0)
                                            ).then_inc(pair_loaded[n // 2].sem, 16)

            for l in range(DEPTH):
                if l:
                    pool.wait_ge(*logits(l - 1, 1))
                    pool.wait_ge(*ranks(l - 1, 1))
                    pool.wait_ge(*pos_ready(l - 1, 1))
                    load_rows(pool, l)
                else:
                    pool.wait_ge(*mh_done(0, 4))
                    pool.dma_start(mh_dram[:, :], mhT[:, :, :].rearrange("p c m -> p (c m)")).then_inc(mh_stored.sem, 16)
                    pool.wait_ge(*mh_stored(0, 1))
                def masked(buf, sig):
                    d = buf[:, 0:1536].rearrange("p (n s) -> p n s", n=3)[:, :, 0:P]
                    done(pool, nc.gpsimd.tensor_tensor(d, d, strict[:, None, :].broadcast_to([P, 3, P]), ALU.mult), pool_step)
                    d = buf[:, B_AT[3]:B_AT[3] + P]
                    done(pool, nc.gpsimd.tensor_tensor(d, d, strict[:, :], ALU.mult), sig)

                for n in range(H):
                    pool.wait_ge(*b_max(l, n + 1))
                    masked(h_flat[:, 0:1536], b_sp)
                    pool.wait_ge(*b_w(l, 3 * n + 3))
                    masked(h_flat[:, 1280:2816], b_wm)
                    if n >= 2:
                        q = 10 + n
                        p, half, w = split_piece(l, q)
                        hi, lo = split_half(half, w)
                        pool.wait_ge(*w_hi(l, q + 1))
                        done(pool, nc.gpsimd.tensor_tensor(lo, piece_half(p, half, w), hi.bitcast(F32), ALU.subtract), w_lo_pool)
                pool.wait_ge(*g_out(l, 6))
                yb = xn[:, :, 512:768]
                b4 = yb.rearrange("p t (g d) -> p t g d", g=G)
                done(pool, nc.gpsimd.tensor_tensor(b4, b4, stat(240, 16).rearrange("p (t g) -> p t g", t=T)[:, :, :, None]
                                                   .broadcast_to([P, T, G, 64]), ALU.mult), pool_step)
                a, n = ROWS["b_out"]
                done(pool, nc.gpsimd.tensor_tensor(yb, yb, rows[:, None, a:a + n].broadcast_to([P, T, n]), ALU.mult), b_wm)
                if l + 1 < DEPTH:
                    pool.wait_ge(*x_mix(l, 8))
                    pool.dma_start(mg[:, :, :].rearrange("p c m -> p (c m)"), mh_dram[:, :]).then_inc(mh_loaded.sem, 16)

                pool.wait_ge(*norm_xn["ffn"](l, T))
                pool.dma_start(xn_dram[:, :].rearrange("(t p) d -> p t d", p=P), xn[:, :, :]).then_inc(xn_stored.sem, 16)
                pool.wait_ge(*lists_ready(l, 1))
                pool.wait_ge(*xn_stored(l, 1))
                pool.wait_ge(*x_cross(l, 8))

                for e in range(E):
                    if e >= 2:
                        pool.wait_ge(*xg_tp(l, 2 * (e - 1)))
                    pool.indirect_dma_start(out=xg[:, e % 2, :], out_offset=None, in_=xn_dram[:, :],
                                            in_offset=bass.IndirectOffsetOnAxis(ap=lists[:, e:e + 1], axis=0)
                                            ).then_inc(gathered[e % 2].sem, 16)
                pool.wait_ge(*pos_ready(l, 1))
                more = pool.value_load(over[0:1, 0:1], min_val=0, max_val=1)
                with pool.If(more > 0):
                    for r in range(T):
                        pool.dma_start(list_dram[r * P * E:(r + 1) * P * E, :].rearrange("(s e) o -> s (e o)", e=E),
                                       zero_i[:, :]).then_inc(list_written[l].sem, 16)
                    pool.wait_ge(*list_written[l](0, T))
                    for n in range(2 * T):
                        pool.indirect_dma_start(out=list_dram[:, :], out_offset=bass.IndirectOffsetOnAxis(ap=pos_list[:, n:n + 1], axis=0),
                                                in_=tok_id[:, n // 2:n // 2 + 1], in_offset=None).then_inc(list_written[l].sem, 16)
                    pool.wait_ge(*list_written[l](0, 3 * T))
                    pool.wait_ge(*y_stored[0](l, E // 2))
                    pool.wait_ge(*y_stored[1](l, E // 2))
                    with pool.Fori(0, E) as e:
                        with pool.Fori(0, 3) as r:
                            pool.wait_ge(over_pe[l].sem, e * 15 + r * 5 + 1)
                            src = list_dram.rearrange("(r s e) o -> e r s o", r=T, e=E)
                            pool.dma_start(over_ids[:, :], src[e, r + 1],
                                           allow_slow_non_contiguous=True).then_inc(over_ids_in[l].sem, 16)
                            pool.wait_ge(over_ids_in[l].sem, e * 48 + r * 16 + 16)
                            pool.sem_inc(over_go[l].sem, 1)
                            pool.indirect_dma_start(out=xg[:, 0, :], out_offset=None, in_=xn_dram[:, :],
                                                    in_offset=bass.IndirectOffsetOnAxis(ap=over_ids[:, 0:1], axis=0)
                                                    ).then_inc(over_x[l].sem, 16)
                    pool.wait_ge(*over_y[l](0, OVER))
                    combine(l, y_dram[:, :])
                with pool.Else():
                    combine(l, y_dram[0:E * P, :])
                pool.end_ifs()
            pool.wait_ge(*lists_ready(DEPTH - 1, 1))
            pool.dma_start(rows[:, 0:D], norm_final.partition_broadcast(P)).then_inc(rows_loaded[DEPTH].sem, 16)

        @block.scalar
        def _(act):
            def step(ins):
                done(act, ins, act_step)

            def rstd_seed(n, width, sig, at=0):
                step(nc.scalar.activation(stat(SEED + at, n), stat(SS + at, n), ACT.Ln, bias=eps_col[:, :], scale=1.0 / width))
                done(act, nc.scalar.activation(stat(SEED + at, n), stat(SEED + at, n), ACT.Exp, scale=-0.5), sig)

            def norm_tile(name, t):
                step(nc.scalar.activation(xn[:, t, :], X[:, t, :], ACT.Square, accum_out=stat(SS + t)))
                rstd_seed(1, D, norm_seed[name], t)

            def norm_high_tile(l, t):
                for c in range(C):
                    act.wait_ge(*norm_tp["mix"](l, 2 * t + 1 + c // 4))
                    ins = nc.scalar.activation(hT_r[:, 0, c, t * P:(t + 1) * P], bank[2 * t + c // 4][:, (c % 4) * P:(c % 4 + 1) * P],
                                               ACT.Copy, scale=gains[:, l, 0, c:c + 1])
                    ins.then_inc(norm_act["mix"].sem, 1)
                    norm_act["mix"].count += 1

            def norm_evac_tile(l, name, g, t, b):
                act.wait_ge(*norm_tp[name](l, 2 * t + 2))
                for c in range(4, C):
                    ins = nc.scalar.activation(hT[:, c, t * P:(t + 1) * P], bank[b][:, (c - 4) * P:(c - 3) * P], ACT.Copy,
                                               scale=gains[:, l, g, c:c + 1])
                    if c < C - 1:
                        ins.then_inc(act_step.sem, 1)
                        act_step.count += 1
                done(act, ins, norm_act[name])

            def group_seed(l, k, n, width):
                act.wait_ge(*g_ss(l, k + 1))
                rstd_seed(n, width, g_seed)

            def group_norm(l, k, src, tmp, n, width):
                done(act, nc.scalar.activation(tmp, src, ACT.Square), g_sq)
                group_seed(l, k, n, width)

            act.dma_start(mraw[:, :, :], mem[0].rearrange("(t p) d -> p t d", p=P)).then_inc(mem_loaded.sem, 16)
            act.dma_start(pos_i[:, :], positions[0].rearrange("(t p) -> p t", p=P),
                          allow_slow_non_contiguous=True).then_inc(gains_loaded.sem, 16)
            for n, g in enumerate((norm_mix, norm_cross, norm_ffn, norm_mem)):
                act.dma_start(gains[:, :, n, :], g.rearrange("l (p c) -> p l c", c=C)).then_inc(gains_loaded.sem, 16)
            nc.scalar.preload_act_table_set("natural_log_exp_and_others")
            act.wait_ge(*mem_loaded(0, 1))
            for t in range(MT):
                step(nc.scalar.activation(mn[:, t, :], mraw[:, t, :], ACT.Square, accum_out=stat(SS + 8 + t)))
            act.wait_ge(*eps_made(0, 1))
            rstd_seed(MT, D, mem_seed, 8)
            act.wait_ge(*x_loaded(0, T))
            for t in range(T):
                norm_tile("mix", t)
            load_rows(act, 0)

            def memory_keys(l):
                for j in range(2):
                    act.wait_ge(*kv(l, j + 1))
                    done(act, nc.scalar.activation(kmT[:, j, :], bank[2 + j][:, 0:M], ACT.Copy), k_out)

            def split_high(l, q):
                p, half, n = split_piece(l, q)
                wait_piece(act, p)
                wait_split_free(act, l, q)
                done(act, nc.scalar.activation(split_half(half, n)[0], piece_half(p, half, n), ACT.Copy), w_hi)

            act.wait_ge(*gains_loaded(0, 5))
            for l in range(DEPTH):
                if l == 0:
                    split_high(0, 0)
                    split_high(0, 1)
                    memory_keys(0)
                else:
                    nc.scalar.preload_act_table_set("natural_log_exp_and_others")
                    act.wait_ge(*xn_stored(l - 1, 1))
                    split_high(l, 0)
                    split_high(l, 1)
                    for t in range(T):
                        act.wait_ge(*x_moe(l - 1, 2 * t + 2))
                        norm_tile("mix", t)
                        if t:
                            norm_high_tile(l, t - 1)
                for t in range(T) if l == 0 else (T - 1,):
                    norm_high_tile(l, t)
                squares = sq_c.rearrange("p (t n) -> p t n", t=T)
                split_high(l, 2)
                for t in range(T):
                    act.wait_ge(*proj_dve(l, t + 1))
                    done(act, nc.scalar.activation(cuv[:, t, 0:256], bank[t][:, 256:512], ACT.Gelu_apprx_tanh), proj_act)
                split_high(l, 3)
                split_high(l, 4)
                for t in range(T):
                    act.wait_ge(*proj(l, 4 + t + 1))
                    done(act, nc.scalar.activation(cuv[:, t, 256:512], bank[4 + t][:, 0:256], ACT.Gelu_apprx_tanh), proj_act)
                split_high(l, 5)
                if l == 0:
                    act.wait_ge(*angles(0, 1))
                    done(act, nc.scalar.activation(cs[:, :, :, :], cs[:, :, :, :], ACT.Sin), rope)
                nc.scalar.preload_act_table_set("natural_log_exp_and_others")
                group_norm(l, 0, cuv[:, :, 256:512], squares, 16, 64)
                split_high(l, 6)
                for t in range(T):
                    act.wait_ge(*proj(l, 8 + t + 1))
                    done(act, nc.scalar.activation(xn[:, t, 0:512], bank[t][:, :], ACT.Copy), proj_act)
                split_high(l, 7)
                act.wait_ge(*lam_sum(l, 1))
                done(act, nc.scalar.activation(stat(LAM + 2, 2), stat(LAM, 2), ACT.Exp), lam_exp)
                split_high(l, 8)
                act.wait_ge(*c_out(l, 2))
                done(act, nc.scalar.activation(squares, cuv[:, :, 0:256], ACT.Square), g_sq)
                for t in range(T):
                    act.wait_ge(*proj(l, 12 + t + 1))
                    done(act, nc.scalar.activation(xn[:, t, 512:1024], bank[4 + t][:, :], ACT.Copy), proj_act)
                split_high(l, 9)
                group_seed(l, 1, 16, 64)
                split_high(l, 10)
                split_high(l, 11)
                act.wait_ge(*rotated(l, T))
                for t in range(T):
                    act.wait_ge(*proj(l, 20 + t + 1))
                    done(act, nc.scalar.activation(bT[:, t, :], bank[4 + t][:, :], ACT.Copy,
                                                   scale=0.125 if t < 2 else 1.0), proj_act)
                for cc in range(0, 8, 2):
                    act.wait_ge(*a_tr(l, cc + 1))
                    done(act, nc.scalar.activation(aT[:, cc, :], bank[cc][:, :], ACT.Copy), aT_act)
                act.wait_ge(*g_out(l, 2))

                def a_step(i):
                    if i < U:
                        t, n = i // H, P * (i // H + 1)
                        if i >= 3:
                            act.wait_ge(*a_tp(l, i - 2))
                        for m in range(2):
                            act.wait_ge(*a_max(l, 2 * i + m + 1))
                            o = pa1[i % 2] if m else pa0[i % 3]
                            done(act, nc.scalar.activation(o[:, 0:n], bank[(2 * i + m) % 3][:, 0:n], ACT.Exp,
                                                           bias=stat(MAXA + 2 * i + m), scale=0.125,
                                                           accum_out=stat(SUMA + 2 * i + m)), a_exp)
                    u = i - 2
                    if 0 <= u < U:
                        n = P * (u // H + 1)
                        act.wait_ge(*a_tp(l, u + 1))
                        if u >= 2:
                            act.wait_ge(*a_pv(l, u - 1))
                        done(act, nc.scalar.activation(pT[:, u % 2, 0:n], bank[4][:, 0:n], ACT.Copy), a_pt)

                def a_norm(i):
                    if i >= 7 and (i - 7) % H == 0 and (i - 7) // H < T - 1:
                        t = (i - 7) // H
                        act.wait_ge(*a_out(l, t + 1))
                        done(act, nc.scalar.activation(sq, xn[:, t, 0:512], ACT.Square), g_sq)
                    if i >= 8 and (i - 8) % H == 0 and (i - 8) // H < T - 1:
                        group_seed(l, 2 + (i - 8) // H, H, P)
                    if i == STEPS - 1:
                        act.wait_ge(*g_out(l, 6))
                        act.wait_ge(*a_pv(l, U))
                        for h in range(H):
                            r = slice(h * P, (h + 1) * P)
                            step(nc.scalar.activation(sq[:, r], bank[5][:, r], ACT.Square, accum_out=stat(SS + h)))
                        rstd_seed(H, P, g_seed)
                    if i == 16:
                        act.wait_ge(*b_out(l, H))
                        group_norm(l, 5, xn[:, :, 512:768], cut(h_flat, 1280, T, 256), 16, 64)

                def b_step(i):
                    h, part = i // 4, i % 4
                    if h < H and part == 0:
                        for j, (a, n) in enumerate(B_JOB):
                            act.wait_ge(*b_min(l, 3 * h + j + 1))
                            step(nc.scalar.activation(sp_buf[:, a:a + n], sp_buf[:, a:a + n], ACT.Exp))
                            done(act, nc.scalar.activation(sp_buf[:, a:a + n], sp_buf[:, a:a + n], ACT.Ln, bias=1.0), b_ln)
                    if h < H and part == 2:
                        for j, (a, n) in enumerate(B_JOB):
                            act.wait_ge(*b_sfx(l, 3 * h + j + 1))
                            if h and j == 0:
                                act.wait_ge(*b_pv(l, h))
                            done(act, nc.scalar.activation(w_buf[:, a:a + n], bank[(6, 7, 3)[j]][:, 0:n], ACT.Exp), b_w)

                for i in range(STEPS):
                    a_step(i)
                    a_norm(i)
                    b_step(i)
                    if i in (8, 10):
                        split_high(l, 8 + i // 2)

                for c in range(C):
                    act.wait_ge(*mix_tp(l, c + 1))
                    done(act, nc.scalar.activation(hT_r[:, 0, c, :], bank[c][:, :], ACT.Copy), mixT_hi)
                split_high(l, 14)
                split_high(l, 15)

                for t in range(T):
                    act.wait_ge(*x_mix(l, 4 + t + 1))
                    norm_tile("cross", t)
                    if t:
                        norm_evac_tile(l, "cross", 1, t - 1, 2 * t - 1)
                norm_evac_tile(l, "cross", 1, T - 1, 2 * T - 1)
                for j in range(2):
                    act.wait_ge(*cq(l, j + 1))
                    done(act, nc.scalar.activation(cqT[:, j, :], bank[j][:, :], ACT.Copy), cq_out)

                def cross_exp(t):
                    act.wait_ge(*c_max(l, t + 1))
                    if t >= 2:
                        act.wait_ge(*c_tp(l, 2 * (t - 1)))
                    for h in range(H):
                        ins = nc.scalar.activation(pc[:, t % 2, h, :], bank[2 + 2 * (t % 2) + h % 2][:, (h // 2) * M:(h // 2 + 1) * M],
                                                   ACT.Exp, bias=stat(MAXC + H * t + 2 * (h % 2) + h // 2), scale=0.125,
                                                   accum_out=stat(SUMC + H * t + h))
                        done(act, ins, c_exp if h == H - 1 else act_step)

                cross_exp(0)
                cross_exp(1)
                for i in range(T + 4):
                    if i < T:
                        act.wait_ge(*c_tp(l, 2 * i + 1))
                        if i >= 2:
                            act.wait_ge(*c_pv(l, i - 1))
                        done(act, nc.scalar.activation(pcT[:, i % 2, 0:512], bank[6][:, :], ACT.Copy), c_pt_act)
                    if i + 2 < T:
                        cross_exp(i + 2)
                    t = i - 2
                    if 0 <= t < T:
                        act.wait_ge(*c_otp(l, t + 1))
                        done(act, nc.scalar.activation(ocT[:, :, t * P:(t + 1) * P],
                                                       bank[t % 2][:, 256:512].rearrange("p (c n) -> p c n", c=2), ACT.Copy), c_ot)
                    t = i - 3
                    if 0 <= t < T:
                        act.wait_ge(*x_cross(l, 2 * t + 2))
                        norm_tile("ffn", t)
                    t = i - 4
                    if 0 <= t < T:
                        norm_evac_tile(l, "ffn", 2, t, (3, 7)[t % 2])

                act.wait_ge(*r_max(l, 1))
                done(act, nc.scalar.activation(cut(rt, R_EG, T, G), cut(rt, R_EG, T, G), ACT.Exp), r_exp)
                act.wait_ge(*r_max(l, 2))
                done(act, nc.scalar.activation(cut(rt, R_E2, T), cut(rt, R_E2, T), ACT.Exp), r_exp)
                if l + 1 < DEPTH:
                    memory_keys(l + 1)
                nc.scalar.preload_act_table_set("silu_and_others")

                def moe_step(k, a, gu=True, dn=True):
                    i = 2 * k + a
                    if dn and gu:
                        p = down_piece(l, a)
                        wait_piece(act, p, k)
                        if a >= 2:
                            act.wait_ge(*down(l, 2 * i - 2))
                        for n in range(2):
                            r = slice(n * PW // 2, (n + 1) * PW // 2)
                            nc.scalar.activation(down_r[0][:, r], piece(p)[:, r], ACT.Copy).then_inc(d_hi.sem, 1)
                    if dn:
                        act.wait_ge(*act_tp(l, i))
                        o = actT_r[:, (a - 1) % 2, 0, :] if gu else actT[:, (a - 1) % 2, :]
                        nc.scalar.activation(o, bank[7][:, :], ACT.Copy).then_inc(actT_out.sem, 1)
                    if gu:
                        act.wait_ge(*gate_up(l, i + 1))
                        if a >= 2:
                            act.wait_ge(*act_ready(l, i - 1))
                        nc.scalar.activation(sg[:, a % 2, :], bank[2 * (a % 2)][:, :], ACT.Silu).then_inc(silu_done.sem, 1)
                    if dn:
                        s = (a - 1) % 2
                        if a >= 3:
                            act.wait_ge(*y_stored[s](l, k + (a - 1) // 2))
                        for n in range(2):
                            act.wait_ge(*down(l, 2 * i - 1 + n))
                            nc.scalar.activation(yo[:, s, 512 * n:512 * n + 512], bank[4 + n][:, :], ACT.Copy).then_inc(y_out.sem, 1)
                        act.wait_ge(*y_out(l, 2 * i))
                        act.dma_start(y_first[i - 1], yo[:, s, :]).then_inc(y_stored[s].sem, 16)

                act.wait_ge(*pos_ready(l, 1))
                
                moe_step(0, 0, dn=False)
                moe_step(0, 1)
                moe_step(0, 2)
                with act.Fori(0, 6) as k:
                    moe_step(k, 3)
                    moe_step(k, 4)
                moe_step(0, 15)
                moe_step(0, 16, gu=False)
                more = act.value_load(over[0:1, 0:1], min_val=0, max_val=1)
                with act.If(more > 0):
                    act.wait_ge(*y_stored[0](l, E // 2))
                    with act.Fori(0, E) as e:
                        with act.Fori(0, 3) as r:
                            n = 3 * e + r
                            oa = over_act[l].sem
                            act.wait_ge(over_pe[l].sem, 5 * n + 1 + 3)
                            nc.scalar.activation(sg[:, 0, :], bank[0][:, :], ACT.Silu).then_inc(oa, 1)
                            act.wait_ge(over_pe[l].sem, 5 * n + 1 + 4)
                            nc.scalar.activation(actT[:, 0, :], bank[7][:, :], ACT.Copy).then_inc(oa, 1)
                            act.wait_ge(over_pe[l].sem, 5 * n + 1 + 5)
                            for q in range(2):
                                nc.scalar.activation(yo[:, 0, 512 * q:512 * q + 512], bank[4 + q][:, :], ACT.Copy).then_inc(oa, 1)
                            act.wait_ge(oa, 4 * n + 4)
                            act.dma_start(y_over[e, r], yo[:, 0, :]).then_inc(over_y[l].sem, 16)
                            act.wait_ge(over_y[l].sem, 16 * n + 16)
                act.end_ifs()

            act.wait_ge(*xn_stored(DEPTH - 1, 1))
            nc.scalar.preload_act_table_set("natural_log_exp_and_others")
            for t in range(T):
                act.wait_ge(*x_moe(DEPTH - 1, 2 * t + 2))
                norm_tile("mix", t)
            for t in range(T):
                act.wait_ge(*out_ready(0, t + 1))
                act.dma_start(out[0, t * P:(t + 1) * P, :], X[:, t, :]).then_inc(out_stored.sem, 16)
            act.wait_ge(*out_stored(0, T))

        @block.vector
        def _(dve):
            def step(ins):
                done(dve, ins, dve_step)

            def scale_(o, i, s1, s2=None, op0=ALU.mult, op1=ALU.add):
                return nc.vector.tensor_scalar(o, i, s1, s2, op0, *([] if s2 is None else [op1]))

            def tt(o, a, b, op=ALU.mult):
                return nc.vector.tensor_tensor(o, a, b, op)

            def newton(n, width, at=0, sig=None, o=None):
                r, t_ = stat(SEED + at, n), stat(TMP + at, n)
                step(scale_(t_, stat(SS + at, n), 1.0 / width, EPS))
                step(tt(t_, t_, r))
                step(tt(t_, t_, r))
                step(scale_(t_, t_, -0.5, 1.5))
                done(dve, tt(r if o is None else stat(o, n), r, t_), sig or dve_step)

            def norm_tile(l, name, t):
                dve.wait_ge(*norm_seed[name](l, t + 1))
                newton(1, D, t)
                done(dve, scale_(xn[:, t, :], X[:, t, :], stat(SEED + t)), norm_xn[name])

            def norm_low_tile(l, t):
                s = slice(t * P, (t + 1) * P)
                for c in range(C):
                    if c % 4 == 0:
                        dve.wait_ge(*norm_act["mix"](l, C * t + c + 4))
                    ins = nc.vector.scalar_tensor_tensor(hT_r[:, 1, c, s], bank[2 * t + c // 4][:, (c % 4) * P:(c % 4 + 1) * P],
                                                         gains[:, l, 0, c:c + 1], hT_r[:, 0, c, s].bitcast(F32),
                                                         ALU.mult, ALU.subtract)
                    if c < C - 1:
                        ins.then_inc(dve_step.sem, 1)
                        dve_step.count += 1
                done(dve, ins, norm_dve["mix"])

            def split_low(l, q):
                p, half, n = split_piece(l, q)
                hi, lo = split_half(half, n)
                dve.wait_ge(*w_hi(l, q + 1))
                wait_split_free(dve, l, q)
                done(dve, tt(lo, piece_half(p, half, n), hi.bitcast(F32), ALU.subtract), w_lo_dve)

            def norm_evac_tile(l, name, g, t, b):
                dve.wait_ge(*norm_tp[name](l, 2 * t + 1))
                done(dve, tt(hT[:, 0:4, t * P:(t + 1) * P], bank[b][:, :].rearrange("p (c s) -> p c s", c=4),
                             gains[:, l, g, 0:4][:, :, None].broadcast_to([P, 4, P])), norm_dve[name])

            def group_sums(l, k, tmp, n):
                dve.wait_ge(*g_sq(l, k + 1))
                done(dve, nc.vector.tensor_reduce(stat(SS, n), tmp, AX.X, ALU.add), g_ss)

            def group_scale(l, k, view, n, width, outer, gain, inner, factor=1.0):
                dve.wait_ge(*g_seed(l, k + 1))
                newton(n, width)
                r = stat(SEED, n)
                if outer:
                    r = r.rearrange("p (t g) -> p t g", t=outer)[:, :, :, None].broadcast_to([P, outer, n // outer, width])
                    step(tt(view, view, r))
                    done(dve, tt(inner, inner, gain[:, None, :].broadcast_to([P, outer, inner.shape[2]])), g_out)
                else:
                    step(tt(view, view, r[:, :, None].broadcast_to([P, n, width])))
                    done(dve, nc.vector.scalar_tensor_tensor(view, view, factor, gain[:, None, :].broadcast_to([P, n, width]),
                                                             ALU.mult, ALU.mult), g_out)

            def row(name):
                a, n = ROWS[name]
                return rows[:, a:a + n]

            def rotary_angles():
                dve.wait_ge(*gains_loaded(0, 5))
                posf = stat(240, T)
                step(nc.vector.tensor_copy(posf, pos_i[:, :]))
                inv = (np.float32(1.0) / np.power(np.float32(ROPE_THETA), np.arange(0, ROPE_DIM, 2, dtype=np.float32) / np.float32(ROPE_DIM))).astype(np.float32)
                ang, turns = cut(rot[:, 0, :], 0, T, HALF), cut(rot[:, 1, :], 0, T, HALF)
                for i in range(HALF):
                    step(scale_(ang[:, :, i], posf, float(inv[i])))
                two_pi = 2 * math.pi
                p1 = 6.28125
                p2 = 0.0019350051879882812
                p3 = two_pi - p1 - p2
                magic = 12582912.0
                for w, (off, shift) in enumerate(((0.25, math.pi / 2), (0.0, 0.0))):
                    step(scale_(turns, ang, 1 / two_pi, off))
                    step(scale_(turns, turns, magic, None, ALU.add))
                    step(scale_(turns, turns, magic, None, ALU.subtract))
                    o = cs[:, w, :, :]
                    step(nc.vector.scalar_tensor_tensor(o, turns, -p1, ang, ALU.mult, ALU.add))
                    step(nc.vector.scalar_tensor_tensor(o, turns, -p2, o, ALU.mult, ALU.add))
                    step(nc.vector.scalar_tensor_tensor(o, turns, -p3, o, ALU.mult, ALU.add))
                    step(scale_(o, o, shift, None, ALU.add))
                    done(dve, scale_(o, o, 3.1415925, -3.1415925, ALU.min, ALU.max), angles if w else dve_step)

            done(dve, nc.vector.memset(eps_col[:, :], EPS), eps_made)
            dve.wait_ge(*mem_seed(0, 1))
            newton(MT, D, 8)
            for t in range(MT):
                done(dve, scale_(mn[:, t, :], mraw[:, t, :], stat(SEED + 8 + t)), mem_norm)
            for j in range(4):
                dve.wait_ge(*mem_tp(0, j + 1))
                done(dve, nc.vector.tensor_copy(cut(work, 512 * j, 512), bank[j][:, :]), mh_done)

            def memory_gain(l, src):
                done(dve, tt(mg[:, :, :], src[:, :, :], gains[:, l, 3, :][:, :, None].broadcast_to([P, C, M])), mg_ready)

            def memory_values(l):
                for t in range(MT):
                    dve.wait_ge(*kv(l, 2 + t + 1))
                    done(dve, nc.vector.tensor_copy(vm[:, t, :], bank[4 + t][:, 0:256]), v_out)

            dve.wait_ge(*gains_loaded(0, 5))
            memory_gain(0, mhT)
            for t in range(T):
                norm_tile(0, "mix", t)
            split_low(0, 0)
            split_low(0, 1)
            memory_values(0)

            for l in range(DEPTH):
                if l == 0:
                    dve.wait_ge(*mh_stored(0, 1))
                    for t in range(T):
                        norm_low_tile(0, t)
                    rotary_angles()
                dve.wait_ge(*rows_loaded[l](0, 11))
                a = ROWS["lam"][0]
                step(tt(rot[:, 0, :], rows[:, a:a + 128], rows[:, a + 128:a + 256]))
                done(dve, nc.vector.tensor_reduce(stat(LAM, 2), cut(rot[:, 0, :], 0, 2, 64), AX.X, ALU.add), lam_sum)
                squares = sq_c.rearrange("p (n d) -> p n d", d=64)
                split_low(l, 2)
                for t in range(T):
                    dve.wait_ge(*proj(l, t + 1))
                    done(dve, nc.vector.tensor_copy(bv[:, t, :], bank[t][:, 0:256]), proj_dve)
                split_low(l, 3)
                split_low(l, 4)
                dve.wait_ge(*ws_tr(l, 1))
                done(dve, tt(wsT[:, :, :], bank[0][:, :].rearrange("p (g t) -> p g t", g=G),
                             keep[:, None, :].broadcast_to([P, G, P])), ws_ready)
                split_low(l, 5)
                group_sums(l, 0, squares, 16)
                group_scale(l, 0, cuv[:, :, 256:512].rearrange("p t (g d) -> p t g d", g=G), 16, 64, T, row("sgu"), cuv[:, :, 256:512])
                for q in (6, 7, 8):
                    split_low(l, q)
                for j in range(2):
                    dve.wait_ge(*c_mm(l, j + 1))
                    u2 = cuv[:, 2 * j:2 * j + 2, 0:256]
                    vu = cuv[:, 2 * j:2 * j + 2, 256:512]
                    ps = bank[j][:, :].rearrange("p (t g d) -> p t g d", t=2, g=G)
                    step(tt(vu.rearrange("p t (g d) -> p t g d", g=G), ps,
                            bsp[:, None, :, None].broadcast_to([P, 2, G, 64]), ALU.add))
                    done(dve, tt(u2, u2, vu), c_out)
                group_sums(l, 1, squares, 16)
                split_low(l, 9)
                dve.wait_ge(*g_seed(l, 2))
                newton(16, 64)
                c4 = cuv[:, :, 0:256].rearrange("p t (g d) -> p t g d", g=G)
                step(tt(c4, c4, stat(SEED, 16).rearrange("p (t g) -> p t g", t=T)[:, :, :, None].broadcast_to([P, T, G, 64])))
                if l == 0:
                    dve.wait_ge(*rope(0, 1))
                for t in range(T):
                    dve.wait_ge(*proj_act(l, 12 + t + 1))
                    v = xn[:, t, :].rearrange("p (n d) -> p n d", d=64)
                    lo, hi = v[:, :, 0:HALF], v[:, :, HALF:ROPE_DIM]
                    co = cs[:, 0, t, :][:, None, :].broadcast_to([P, 16, HALF])
                    si = cs[:, 1, t, :][:, None, :].broadcast_to([P, 16, HALF])
                    q = [cut(rot[:, n, :], 0, 16, HALF) for n in range(4)]
                    step(tt(q[0], lo, co))
                    step(tt(q[1], hi, si))
                    step(tt(q[2], hi, co))
                    step(tt(q[3], lo, si))
                    step(tt(lo, q[0], q[1], ALU.subtract))
                    done(dve, tt(hi, q[2], q[3], ALU.add), rotated)
                split_low(l, 10)
                dve.wait_ge(*lam_exp(l, 1))
                lam_init = 0.8 - 0.6 * math.exp(-0.3 * l)
                step(tt(stat(LAM + 4), stat(LAM + 2), stat(LAM + 3), ALU.subtract))
                done(dve, scale_(stat(LAM + 5), stat(LAM + 4), -1.0, -lam_init), lam_ready)
                for t in range(T):
                    dve.wait_ge(*proj(l, 16 + t + 1))
                    done(dve, nc.vector.tensor_copy(av[:, t, :], bank[t][:, :]), proj_dve)
                split_low(l, 11)
                for cc in range(1, 8, 2):
                    dve.wait_ge(*a_tr(l, cc + 1))
                    done(dve, nc.vector.tensor_copy(aT[:, cc, :], bank[cc][:, :]), aT_dve)
                done(dve, tt(xn[:, :, 768:1024], cuv[:, :, 0:256], row("c_out")[:, None, :].broadcast_to([P, T, 256])), g_out)

                def a_step(i):
                    if i < U:
                        n = P * (i // H + 1)
                        for m in range(2):
                            dve.wait_ge(*a_scores(l, 2 * i + m + 1))
                            step(nc.vector.reduce_max(stat(MAXA + 2 * i + m), bank[(2 * i + m) % 3][:, 0:n], AX.X))
                            done(dve, scale_(stat(MAXA + 2 * i + m), stat(MAXA + 2 * i + m), -0.125), a_max)
                    u = i - 1
                    if 0 <= u < U:
                        n = P * (u // H + 1)
                        p0, p1 = pa0[u % 3][:, 0:n], pa1[u % 2][:, 0:n]
                        dve.wait_ge(*a_exp(l, 2 * u + 2))
                        r = RLA + 2 * (u % 16)
                        step(nc.vector.reciprocal(stat(r, 2), stat(SUMA + 2 * u, 2)))
                        step(tt(stat(r + 1), stat(r + 1), stat(LAM + 5)))
                        step(scale_(p1, p1, stat(r + 1)))
                        done(dve, nc.vector.scalar_tensor_tensor(p0, p0, stat(r), p1, ALU.mult, ALU.add), a_comb)

                def a_norm(i):
                    if i >= 6 and (i - 6) % H == 0 and (i - 6) // H < T - 1:
                        t = (i - 6) // H
                        dve.wait_ge(*a_pv(l, H * t + H))
                        done(dve, nc.vector.tensor_copy(xn[:, t, 0:512], bank[5][:, :]), a_out)
                    if i >= 7 and (i - 7) % H == 0 and (i - 7) // H < T - 1:
                        group_sums(l, 2 + (i - 7) // H, sq.rearrange("p (h d) -> p h d", h=H), H)
                    if i == STEPS - 1:
                        dve.wait_ge(*g_seed(l, 7))
                        newton(H, P)
                        o = xn[:, T - 1, 0:512].rearrange("p (h d) -> p h d", h=H)
                        step(tt(o, bank[5][:, :].rearrange("p (h d) -> p h d", h=H), stat(SEED, H)[:, :, None].broadcast_to([P, H, P])))
                        done(dve, nc.vector.scalar_tensor_tensor(o, o, 1.0 - lam_init, row("subln")[:, None, :].broadcast_to([P, H, P]),
                                                                 ALU.mult, ALU.mult), g_out)
                    if i in (9, 13, 16):
                        t = (i - 8) // H
                        group_scale(l, 2 + t, xn[:, t, 0:512].rearrange("p (h d) -> p h d", h=H), H, P, 0, row("subln"), None,
                                    1.0 - lam_init)
                    if i == 16:
                        group_sums(l, 5, cut(h_flat, 1280, 16, 64), 16)
                        dve.wait_ge(*g_seed(l, 6))
                        newton(16, 64, 0, g_out, 240)

                def b_copy(i):
                    h, part = i // 4, i % 4
                    if 1 <= h <= H and part == 0:
                        g = h - 1
                        dve.wait_ge(*b_pv(l, h))
                        done(dve, nc.vector.tensor_copy(xn[:, :, 512 + 64 * g:576 + 64 * g],
                                                        bank[3][:, 256:512].rearrange("p (t d) -> p t d", t=T)), b_out)

                def b_step(i):
                    h, part = i // 4, i % 4
                    if h < H and part == 0:
                        for j, (a, n) in enumerate(B_JOB):
                            dve.wait_ge(*b_z(l, 3 * h + j + 1))
                            done(dve, scale_(sp_buf[:, a:a + n], bank[(6, 7, 3)[j]][:, 0:n], 17.0, None, ALU.min), b_min)
                    if h < H and part == 1:
                        for j, (a, n) in enumerate(B_JOB):
                            dve.wait_ge(*b_ln(l, 3 * h + j + 1))
                            done(dve, tt(sp_buf[:, a:a + n], bank[(6, 7, 3)[j]][:, 0:n], sp_buf[:, a:a + n], ALU.max),
                                 b_max if j == 2 else dve_step)

                for i in range(STEPS):
                    b_copy(i)
                    a_step(i)
                    b_step(i)
                    a_norm(i)
                for c in range(C):
                    dve.wait_ge(*mixT_hi(l, c + 1))
                    done(dve, tt(hT_r[:, 1, c, :], bank[c][:, :], hT_r[:, 0, c, :].bitcast(F32), ALU.subtract), mixT_lo)
                split_low(l, 14)
                for j in range(8):
                    t, n = j % T, j // T
                    if j == T:
                        split_low(l, 15)
                    dve.wait_ge(*o_mm(l, j + 1))
                    xs = X[:, t, 512 * n:512 * n + 512]
                    done(dve, tt(xs, xs, bank[j][:, :], ALU.add), x_mix)
                    if n:
                        if t:
                            norm_tile(l, "cross", t - 1)
                        if t >= 2:
                            norm_evac_tile(l, "cross", 1, t - 2, 2 * t - 4)
                norm_tile(l, "cross", T - 1)
                for t in (T - 2, T - 1):
                    norm_evac_tile(l, "cross", 1, t, 2 * t)

                def cross_max(t):
                    dve.wait_ge(*c_scores(l, t + 1))
                    for j in range(2):
                        step(nc.vector.reduce_max(stat(MAXC + H * t + 2 * j, 2),
                                                  bank[2 + 2 * (t % 2) + j][:, :].rearrange("p (h m) -> p h m", h=2), AX.X))
                    done(dve, scale_(stat(MAXC + H * t, H), stat(MAXC + H * t, H), -0.125), c_max)

                cross_max(0)
                cross_max(1)
                for i in range(T + 4):
                    if i < T:
                        dve.wait_ge(*c_tp(l, 2 * i + 2))
                        if i >= 2:
                            dve.wait_ge(*c_pv(l, i - 1))
                        done(dve, nc.vector.tensor_copy(pcT[:, i % 2, 512:1024], bank[7][:, :]), c_pt_dve)
                        step(nc.vector.reciprocal(stat(RLC + H * i, H), stat(SUMC + H * i, H)))
                    if i + 2 < T:
                        cross_max(i + 2)
                    t = i - 3
                    if 0 <= t < T:
                        for n in range(2):
                            dve.wait_ge(*co_mm(l, 2 * t + n + 1))
                            xs = X[:, t, 512 * n:512 * n + 512]
                            done(dve, tt(xs, xs, bank[4 + n][:, :], ALU.add), x_cross)
                    t = i - 1
                    if 0 <= t < T:
                        dve.wait_ge(*c_pv(l, t + 1))
                        done(dve, tt(oc[:, t % 2, :].rearrange("p (h d) -> p h d", h=H),
                                     bank[t % 2][:, 0:256].rearrange("p (h d) -> p h d", h=H),
                                     stat(RLC + H * t, H)[:, :, None].broadcast_to([P, H, 64])), c_o)
                    t = i - 3
                    if 0 <= t < T:
                        norm_tile(l, "ffn", t)
                    t = i - 4
                    if 0 <= t < T:
                        norm_evac_tile(l, "ffn", 2, t, (2, 6)[t % 2])

                if l + 1 < DEPTH:
                    dve.wait_ge(*mh_loaded(l, 1))
                    memory_gain(l + 1, mg)

                lg = cut(rt, R_LOG, T, G + E)
                eg, e2 = cut(rt, R_EG, T, G), cut(rt, R_E2, T)
                og, el, o1, o2 = (cut(rt, a, T, G) for a in (R_OG, R_EL, R_O1, R_O2))
                tmp = cut(rt, R_TMP, T, G, G)
                pg, gi, i1 = cut(rt, R_PG, T), cut(rt, R_GI, T), cut(rt, R_I, T)
                prod, wide_ = cut(rt, R_PR, T, E), cut(rt, R_W, T, E)
                dve.wait_ge(*logits(l, 1))
                a, n = ROWS["route"]
                step(tt(lg, bank[0][:, 0:T * (G + E)].rearrange("p (t n) -> p t n", t=T),
                        rows[:, None, a:a + n].broadcast_to([P, T, G + E]), ALU.add))

                def over4(v):
                    return v[:, :, None].broadcast_to([P, T, 4])

                def first_max(vals, m, index, onehot):
                    step(nc.vector.tensor_reduce(m, vals, AX.X, ALU.max))
                    step(tt(onehot, vals, over4(m), ALU.is_ge))
                    step(scale_(onehot, onehot, -4.0, 4.0))
                    step(tt(onehot, onehot, iota4[:, None, :].broadcast_to([P, T, 4]), ALU.add))
                    step(nc.vector.tensor_reduce(index, onehot, AX.X, ALU.min))
                    step(tt(onehot, iota4[:, None, :].broadcast_to([P, T, 4]), over4(index), ALU.is_equal))

                gm, m1, m2 = stat(208, T), stat(212, T), stat(216, T)
                first_max(lg[:, :, 0:G], gm, gi, og)
                done(dve, tt(eg, lg[:, :, 0:G], over4(gm), ALU.subtract), r_max)
                step(tt(tmp, lg[:, :, G:].rearrange("p t (g j) -> p t g j", g=G),
                        og[:, :, :, None].broadcast_to([P, T, G, G])))
                step(nc.vector.tensor_reduce(el, tmp.rearrange("p t g j -> p t j g"), AX.X, ALU.add))
                first_max(el, m1, i1, o1)
                step(nc.vector.scalar_tensor_tensor(el, o1, NEG, el, ALU.mult, ALU.add))
                first_max(el, m2, i1, o2)
                done(dve, tt(e2, m2, m1, ALU.subtract), r_max)
                dve.wait_ge(*r_exp(l, 2))
                step(nc.vector.tensor_reduce(pg, eg, AX.X, ALU.add))
                step(nc.vector.reciprocal(pg, pg))
                g1, g2 = gate[:, 0, :], gate[:, 1, :]
                step(scale_(g2, e2, 1.0, None, ALU.add))
                step(nc.vector.reciprocal(g1, g2))
                step(tt(g1, g1, pg))
                step(tt(g2, g1, e2))
                for n, o in enumerate((o1, o2)):
                    step(tt(wide_[:, :, :].rearrange("p t (g j) -> p t g j", g=G), og[:, :, :, None].broadcast_to([P, T, G, G]),
                            o[:, :, None, :].broadcast_to([P, T, G, G])))
                    if n == 0:
                        step(nc.vector.tensor_copy(prod, wide_))
                done(dve, tt(mask_b[:, :, :], prod, wide_, ALU.add), masks)
                dve.wait_ge(*ranks(l, 1))
                rank = bank[1][:, 0:T * E].rearrange("p (t e) -> p t e", t=T)
                e16 = iotaE[:, None, :].broadcast_to([P, T, E])
                es = stat(224, T)
                buf = cut(rt, 384, T, E)
                r_of = (stat(216, T), stat(220, T))
                for n, o in enumerate((prod, wide_)):
                    step(tt(buf, o, rank))
                    step(nc.vector.tensor_reduce(r_of[n], buf, AX.X, ALU.add))
                    for t in range(T):
                        step(scale_(hot[:, n, t, :], slot_b[:, :], r_of[n][:, t:t + 1], None, ALU.is_equal))
                    step(scale_(ids_b[:, n, 0, :, :], o, lane[:, :]))
                    done(dve, tt(ids_b[:, n, 1, :, :], o, tile_base[:, :, :]), hot_ready if n else dve_step)
                dve.wait_ge(*lists_mm(l, 1))
                done(dve, nc.vector.tensor_copy(lists[:, :], bank[0][:, 256:256 + E]), lists_ready)
                for n, o in enumerate((prod, wide_)):
                    rs = r_of[n]
                    step(tt(buf, o, e16))
                    step(nc.vector.tensor_reduce(es, buf, AX.X, ALU.add))
                    step(nc.vector.scalar_tensor_tensor(pos_list.rearrange("p (t k) -> p k t", k=2)[:, n, :], rs, float(E), es, ALU.mult, ALU.add))
                    big, py = stat(232, T), stat(236, T)
                    step(scale_(big, rs, float(P), None, ALU.is_ge))
                    step(scale_(py, es, float(S - 2 * P), float(E * P - P)))
                    step(tt(big, big, py))
                    step(nc.vector.scalar_tensor_tensor(py, es, float(P), rs, ALU.mult, ALU.add))
                    step(tt(pos_y.rearrange("p (t k) -> p k t", k=2)[:, n, :], py, big, ALU.add))
                step(nc.vector.reduce_max(stat(228), bank[1][:, T * E:T * E + E], AX.X))
                done(dve, scale_(over[:, :], stat(228), float(P), None, ALU.is_gt), pos_ready)

                if l + 1 < DEPTH:
                    memory_values(l + 1)

                gain4 = gains[:, l, 2, :]

                def evac_rows(half, slot):
                    return tt(xgT[:, slot, 512 * half:512 * half + 512].rearrange("p (c s) -> p c s", c=4),
                              bank[6][:, :].rearrange("p (c s) -> p c s", c=4),
                              gain4[:, 4 * half:4 * half + 4][:, :, None].broadcast_to([P, 4, P]))

                def moe_step(k, a, gu=True, xt=True):
                    i = 2 * k + a
                    if a >= 1:
                        p = down_piece(l, a)
                        for n in range(2):
                            r = slice(n * PW // 2, (n + 1) * PW // 2)
                            dve.wait_ge(*d_hi(l, 2 * i - 1 + n))
                            tt(down_r[1][:, r], piece(p)[:, r], down_r[0][:, r].bitcast(F32), ALU.subtract).then_inc(d_lo.sem, 1)
                        s = (a - 1) % 2
                        dve.wait_ge(*actT_out(l, i))
                        tt(actT_r[:, s, 1, :], bank[7][:, :], actT_r[:, s, 0, :].bitcast(F32), ALU.subtract).then_inc(actT_lo.sem, 1)
                    if xt:
                        for half in range(2):
                            dve.wait_ge(*xg_tp(l, 2 * (i + 1) + half + 1))
                            evac_rows(half, (a + 1) % 2).then_inc(xg_out.sem, 1)
                    if gu:
                        s, b = a % 2, 2 * (a % 2)
                        dve.wait_ge(*silu_done(l, i + 1))
                        if a >= 2:
                            dve.wait_ge(*act_tp(l, i - 1))
                        tt(act_[:, s, :], sg[:, s, :], bank[b + 1][:, :]).then_inc(act_ready.sem, 1)

                dve.wait_ge(*xn_stored(l, 1))
                moe_step(0, -1, gu=False)
                moe_step(0, 0)
                moe_step(0, 1)
                moe_step(0, 2)
                with dve.Fori(0, 6) as k:
                    moe_step(k, 3)
                    moe_step(k, 4)
                moe_step(0, 15, xt=False)
                more = dve.value_load(over[0:1, 0:1], min_val=0, max_val=1)
                with dve.If(more > 0):
                    with dve.Fori(0, E) as e:
                        with dve.Fori(0, 3) as r:
                            n, od = 3 * e + r, over_dve[l].sem
                            for half in range(2):
                                dve.wait_ge(over_pe[l].sem, 5 * n + 1 + half + 1)
                                evac_rows(half, 0).then_inc(od, 1)
                            dve.wait_ge(over_act[l].sem, 4 * n + 1)
                            tt(act_[:, 0, :], sg[:, 0, :], bank[1][:, :]).then_inc(od, 1)
                dve.end_ifs()
                if l + 1 < DEPTH:
                    split_low(l + 1, 0)
                    split_low(l + 1, 1)
                for t in range(T + 2):
                    if t < T:
                        dve.wait_ge(*pair_loaded[t](l, 2))
                        for c in range(2):
                            done(dve, nc.vector.scalar_tensor_tensor(X[:, t, :], yg[:, 2 * t + c, :], gate[:, c, t:t + 1],
                                                                     X[:, t, :], ALU.mult, ALU.add), x_moe)
                    if 0 < t <= T:
                        norm_tile(l + 1, "mix", t - 1)
                        if l + 1 == DEPTH:
                            if t == 1:
                                dve.wait_ge(*rows_loaded[DEPTH](0, 1))
                            done(dve, tt(X[:, t - 1, :], xn[:, t - 1, :], rows[:, 0:D]), out_ready)
                    if t > 1 and l + 1 < DEPTH:
                        norm_low_tile(l + 1, t - 2)

        @block.tensor
        def _(pe):
            def mm(o, w, v, first=True, last=True):
                return nc.tensor.matmul(o, w, v, start=first, stop=last)

            def use(p, k=0):
                wait_piece(pe, p, k)

            def wide(p, n):
                return piece(p)[:, 0:C * n].rearrange("p (c n) -> p c n", n=n)

            def norm_tile(l, name, t, banks):
                pe.wait_ge(*norm_xn[name](l, t + 1))
                for half in range(2):
                    for c in range(4):
                        ins = nc.tensor.transpose(bank[banks[half]][:, c * P:(c + 1) * P], xn[:, t, 4 * half + c::C], ident[:, :])
                    ins.then_inc(norm_tp[name].sem, 1)

            def split_product(o, tokens, half, n, at=None):
                hi, lo = split_half(half, n)
                for c in range(4):
                    h_ = [hT_r[:, i, 4 * half + c, tokens] for i in range(2)]
                    w_ = [hi[:, c, :], lo[:, c, :]] if at is None else [hi[:, c, at:at + P], lo[:, c, at:at + P]]
                    a, b = (h_, w_) if at is None else (w_, h_)
                    mm(o, a[0], b[0], half == 0 and c == 0, False)
                    mm(o, a[0], b[1], False, False)
                    ins = mm(o, a[1], b[0], False, half == 1 and c == 3)
                return ins

            def memory_keys(l):
                pe.wait_ge(*mg_ready(l, 1))
                w = wide(memory_piece(l), 256)
                use(memory_piece(l))
                for j in range(2):
                    for c in range(C):
                        ins = mm(bank[2 + j][:, 0:M], w[:, c, j * P:(j + 1) * P], mg[:, c, :], c == 0, c == C - 1)
                    ins.then_inc(kv.sem, 1)

            def memory_values(l, tiles=range(MT)):
                w = wide(memory_piece(l) + 1, 256)
                use(memory_piece(l) + 1)
                for t in tiles:
                    for c in range(C):
                        ins = mm(bank[4 + t][:, 0:256], mg[:, c, t * P:(t + 1) * P], w[:, c, :], c == 0, c == C - 1)
                    ins.then_inc(kv.sem, 1)

            pe.wait_ge(*consts_made(0, 11))
            pe.wait_ge(*mem_norm(0, MT))
            for j in range(4):
                for c in (2 * j, 2 * j + 1):
                    for t in range(MT):
                        ins = nc.tensor.transpose(bank[j][:, (c % 2) * M + t * P:(c % 2) * M + (t + 1) * P], mn[:, t, c::C], ident[:, :])
                ins.then_inc(mem_tp.sem, 1)

            pe.wait_ge(*mh_done(0, 4))
            memory_keys(0)
            memory_values(0)
            pe.wait_ge(*k_out(0, 2))
            pe.wait_ge(*v_out(0, 2))

            for l in range(DEPTH):
                f, b = first_piece(l), expert_piece(l)
                norm_tile(l, "mix", 0, (0, 1))
                norm_tile(l, "mix", 1, (2, 3))
                for s, g in enumerate(ORDER):
                    n = 256 if g == 5 else 512
                    for half in range(2):
                        pe.wait_ge(*w_lo(l, 2 * s + half))
                        if half and s == 1:
                            pe.wait_ge(*wr_loaded[l](0, 3))
                            pe.wait_ge(*proj_act(l, 1))
                            for k in range(G):
                                ins = nc.tensor.transpose(bank[0][:, k * P:(k + 1) * P], wsp[:, k, :], ident[:, :])
                            ins.then_inc(ws_tr.sem, 1)
                        if half and s == 3:
                            pe.wait_ge(*proj_act(l, 10))
                            pe.wait_ge(*g_out(l, 1))
                            for t in range(T):
                                for k in range(G):
                                    o = (t % 2) * 256 + k * 64
                                    ins = mm(bank[t // 2][:, o:o + 64], wsT[:, k, :], cuv[:, t, 256 + k * 64:320 + k * 64])
                                if t % 2:
                                    ins.then_inc(c_mm.sem, 1)
                        for t in range(T):
                            j = 4 * s + t
                            if half == 0:
                                if s == 0:
                                    pe.wait_ge(*norm_dve["mix"](l, t + 1))
                                elif s >= 2:
                                    pe.wait_ge(*proj_act(l, j - 7))
                                if s == 2 and t == 0:
                                    pe.wait_ge(*ws_ready(l, 1))
                                if s == 4 and t < 2:
                                    pe.wait_ge(*c_out(l, t + 1))
                            if g == 3:
                                ins = split_product(bank[j % 8][:, :], slice(0, S), half, n, t * P)
                            else:
                                ins = split_product(bank[j % 8][:, 0:n], slice(t * P, (t + 1) * P), half, n)
                            if half:
                                ins.then_inc(proj.sem, 1)
                            elif s == 0 and t < 2:
                                norm_tile(l, "mix", t + 2, (2 * t + 4, 2 * t + 5))
                        if half == 0:
                            ins.then_inc(half_used.sem, 1)
                pe.wait_ge(*rotated(l, T))
                for cc in range(8):
                    if cc < 4:
                        pe.wait_ge(*proj_dve(l, 4 + cc + 1))
                    else:
                        pe.wait_ge(*proj_act(l, 12 + cc + 1))
                    for t in range(T):
                        ins = nc.tensor.transpose(bank[cc][:, t * P:(t + 1) * P], xn[:, t, cc * P:(cc + 1) * P], ident[:, :])
                    ins.then_inc(a_tr.sem, 1)
                pe.wait_ge(*aT_act(l, 4))
                pe.wait_ge(*aT_dve(l, 4))
                if l == 0:
                    pe.wait_ge(*consts_made(0, 16))

                def a_step(i):
                    if i < U:
                        t, h = i // H, i % H
                        n = P * (t + 1)
                        for m in range(2):
                            job = 2 * i + m
                            if job >= 3:
                                pe.wait_ge(*a_exp(l, job - 2))
                            o, r = bank[job % 3], slice(64 * m, 64 * m + 64)
                            mm(o[:, 0:n], aT[r, h, t * P:(t + 1) * P], aT[r, 4 + h, 0:n], True, False)
                            mm(o[:, t * P:n], ident_b[:, :], causal_b[:, :], False, True).then_inc(a_scores.sem, 1)
                    u = i - 2
                    if 0 <= u < U:
                        pe.wait_ge(*a_comb(l, u + 1))
                        if u:
                            pe.wait_ge(*a_pt(l, u))
                        for kb in range(u // H + 1):
                            ins = nc.tensor.transpose(bank[4][:, kb * P:(kb + 1) * P], pa0[u % 3][:, kb * P:(kb + 1) * P], ident[:, :])
                        ins.then_inc(a_tp.sem, 1)
                    u = i - 3
                    if 0 <= u < U:
                        t, h = u // H, u % H
                        pe.wait_ge(*a_pt(l, u + 1))
                        if h == 0 and t:
                            pe.wait_ge(*a_out(l, t))
                        for kb in range(t + 1):
                            ins = mm(bank[5][:, h * P:(h + 1) * P], pT[:, u % 2, kb * P:(kb + 1) * P], av[:, kb, h * P:(h + 1) * P],
                                     kb == 0, kb == t)
                        ins.then_inc(a_pv.sem, 1)

                def b_place(kb):
                    return ((6, 0), (7, 0), (3, 0), (7, 384))[kb]

                def b_step(i):
                    h, part = i // 4, i % 4
                    if h < H and part == 0:
                        if h:
                            pe.wait_ge(*b_w(l, 3 * h))
                        r = slice(64 * (h % 2), 64 * (h % 2) + 64)
                        for kb in (0, 1, 3, 2):
                            bk, o = b_place(kb)
                            if kb == 2 and h:
                                pe.wait_ge(*b_out(l, h))
                            ins = nc.tensor.matmul(bank[bk][:, o:o + S - kb * P], bT[r, 2 + h // 2, kb * P:(kb + 1) * P],
                                                   bT[r, h // 2, kb * P:S], start=kb != 3, stop=False, skip_group_check=True)
                            if kb != 1:
                                ins.then_inc(b_z.sem, 1)
                    if h < H and part == 2:
                        pe.wait_ge(*b_sp(l, h + 1))
                        for kb in (0, 1, 3, 2):
                            bk, o = b_place(kb)
                            for k2 in range(kb, T):
                                n = S - k2 * P
                                ins = nc.tensor.matmul(bank[bk][:, o + (k2 - kb) * P:o + (k2 - kb) * P + n],
                                                       (neg_tri if k2 == kb else neg_one)[:, :], sp_buf[:, B_AT[k2]:B_AT[k2] + n],
                                                       start=False, stop=k2 == T - 1, skip_group_check=True)
                            if kb != 1:
                                ins.then_inc(b_sfx.sem, 1)
                    if h < H and part == 3:
                        pe.wait_ge(*b_wm(l, h + 1))
                        for t in range(T):
                            for kb in range(t + 1):
                                a = B_AT[kb] + (t - kb) * P
                                ins = mm(bank[3][:, 256 + t * 64:320 + t * 64], w_buf[:, a:a + P], bv[:, kb, h * 64:(h + 1) * 64],
                                         kb == 0, kb == t)
                        ins.then_inc(b_pv.sem, 1)

                pe.wait_ge(*lam_ready(l, 1))
                for i in range(STEPS):
                    a_step(i)
                    b_step(i)

                pe.wait_ge(*g_out(l, 7))
                pe.wait_ge(*b_wm(l, H + 1))
                for c in range(C):
                    for t in range(T):
                        ins = nc.tensor.transpose(bank[c][:, t * P:(t + 1) * P], xn[:, t, c::C], ident[:, :])
                    ins.then_inc(mix_tp.sem, 1)
                for g in range(2):
                    for half in range(2):
                        if g == 0:
                            pe.wait_ge(*mixT_lo(l, 4 * half + 4))
                        pe.wait_ge(*w_lo(l, 12 + 2 * g + half))
                        for t in range(T):
                            ins = split_product(bank[4 * g + t][:, :], slice(t * P, (t + 1) * P), half, 512)
                            if half:
                                ins.then_inc(o_mm.sem, 1)
                        if half == 0:
                            ins.then_inc(half_used.sem, 1)
                def cross_norm(t):
                    pe.wait_ge(*x_mix(l, 2 * t + 2))
                    norm_tile(l, "cross", t, (2 * t, 2 * t + 1))

                for t in range(T - 1):
                    cross_norm(t)

                use(f + W_CQ)
                w = wide(f + W_CQ, 256)
                for half in range(2):
                    if half:
                        cross_norm(T - 1)
                    pe.wait_ge(*norm_act["cross"](l, 2 * half + 2))
                    pe.wait_ge(*norm_dve["cross"](l, 2 * half + 2))
                    r = slice(256 * half, 256 * half + 256)
                    for j in range(2):
                        for c in range(C):
                            ins = mm(bank[j][:, r], w[:, c, j * P:(j + 1) * P], hT[:, c, r], c == 0, c == C - 1)
                        if half:
                            ins.then_inc(cq.sem, 1)
                pe.wait_ge(*cq_out(l, 2))

                def scores(t):
                    if t >= 2:
                        pe.wait_ge(*c_exp(l, t - 1))
                    for h in range(H):
                        r = slice(64 * (h % 2), 64 * (h % 2) + 64)
                        ins = mm(bank[2 + 2 * (t % 2) + h % 2][:, (h // 2) * M:(h // 2 + 1) * M], cqT[r, h // 2, t * P:(t + 1) * P],
                                 kmT[r, h // 2, :])
                    ins.then_inc(c_scores.sem, 1)

                wco = piece(f + W_CO)[:, 0:2 * D].rearrange("p (c n) -> p c n", c=2)
                scores(0)
                scores(1)
                for i in range(T + 5):
                    if i < T:
                        pe.wait_ge(*c_exp(l, i + 1))
                        if i:
                            pe.wait_ge(*c_pt_act(l, i))
                            pe.wait_ge(*c_pt_dve(l, i))
                        for h in range(H):
                            for kb in range(MT):
                                ins = nc.tensor.transpose(bank[6 + h // 2][:, ((h % 2) * 2 + kb) * P:((h % 2) * 2 + kb + 1) * P],
                                                          pc[:, i % 2, h, kb * P:(kb + 1) * P], ident[:, :])
                            if h % 2:
                                ins.then_inc(c_tp.sem, 1)
                    if i + 2 < T:
                        scores(i + 2)
                    t = i - 3
                    if 0 <= t < T:
                        pe.wait_ge(*c_ot(l, t + 1))
                        if t == 0:
                            use(f + W_CO)
                            pe.wait_ge(*c_exp(l, T))
                        for n in range(2):
                            if t:
                                pe.wait_ge(*x_cross(l, 2 * t - 1 + n))
                            for c in range(2):
                                ins = mm(bank[4 + n][:, :], ocT[:, c, t * P:(t + 1) * P], wco[:, c, 512 * n:512 * n + 512], c == 0, c == 1)
                            ins.then_inc(co_mm.sem, 1)
                    t = i - 1
                    if 0 <= t < T:
                        pe.wait_ge(*c_pt_act(l, t + 1))
                        pe.wait_ge(*c_pt_dve(l, t + 1))
                        if t >= 2:
                            pe.wait_ge(*c_ot(l, t - 1))
                        for h in range(H):
                            for kb in range(MT):
                                ins = mm(bank[t % 2][:, h * 64:(h + 1) * 64], pcT[:, t % 2, (2 * h + kb) * P:(2 * h + kb + 1) * P],
                                         vm[:, kb, h * 64:(h + 1) * 64], kb == 0, kb == MT - 1)
                        ins.then_inc(c_pv.sem, 1)
                    t = i - 2
                    if 0 <= t < T:
                        pe.wait_ge(*c_o(l, t + 1))
                        for c in range(2):
                            ins = nc.tensor.transpose(bank[t % 2][:, 256 + c * P:256 + (c + 1) * P], oc[:, t % 2, c::2], ident[:, :])
                        ins.then_inc(c_otp.sem, 1)
                    t = i - 4
                    if 0 <= t < T:
                        if t >= 2:
                            pe.wait_ge(*norm_act["ffn"](l, t - 1))
                            pe.wait_ge(*norm_dve["ffn"](l, t - 1))
                        norm_tile(l, "ffn", t, ((2, 3), (6, 7))[t % 2])
                    t = i - 5
                    if 0 <= t < T:
                        if t == 0:
                            pe.wait_ge(*c_ot(l, 3))
                        pe.wait_ge(*norm_act["ffn"](l, t + 1))
                        pe.wait_ge(*norm_dve["ffn"](l, t + 1))
                        for c in range(C):
                            ins = mm(bank[0][:, t * 20:t * 20 + 20], hT[:, c, t * P:(t + 1) * P], wr[:, c, :], c == 0, c == C - 1)
                        if t == T - 1:
                            ins.then_inc(logits.sem, 1)

                if l + 1 < DEPTH:
                    memory_keys(l + 1)
                pe.wait_ge(*masks(l, 1))
                for t in range(T):
                    for t2 in range(t + 1):
                        mm(bank[1][:, t * E:(t + 1) * E], (strict_b if t2 == t else one_b)[:, :], mask_b[:, t2, :], t2 == 0, t2 == t)
                for t in range(T):
                    ins = mm(bank[1][:, T * E:T * E + E], one_b[:, :], mask_b[:, t, :], t == 0, t == T - 1)
                ins.then_inc(ranks.sem, 1)
                if l + 1 < DEPTH:
                    memory_values(l + 1, (0,))
                pe.wait_ge(*hot_ready(l, 1))
                for n in range(16):
                    k, w, t = n // 8, n // 4 % 2, n % 4
                    ins = mm(bank[0][:, 256:256 + E], hot[:, k, t, :], ids_b[:, k, w, t, :], n == 0, n == 15)
                ins.then_inc(lists_mm.sem, 1)
                if l + 1 < DEPTH:
                    memory_values(l + 1, (1,))
                pe.wait_ge(*pos_ready(l, 1))
                if l + 1 < DEPTH:
                    pe.wait_ge(*k_out(l + 1, 2))
                    pe.wait_ge(*v_out(l + 1, 2))

                def rows_half(slot, half):
                    for q in range(4):
                        ins = nc.tensor.transpose(bank[6][:, q * P:(q + 1) * P], xg[:, slot, 4 * half + q::C], ident[:, :])
                    return ins

                def product(o, stationary, w, chunks):
                    for c in range(chunks):
                        ins = mm(o, stationary[:, c * P:(c + 1) * P], w[:, c, :], c == 0, c == chunks - 1)
                    return ins

                def moe_step(k, a, gu=True, xt=True, dn=True):
                    i = 2 * k + a
                    p = b + 3 * a - 1 + (1 if a == 0 else 0)
                    s, bk = a % 2, 2 * (a % 2)
                    if gu:
                        use(p, k)
                        pe.wait_ge(*xg_out(l, 2 * i + 2))
                        if a >= 2:
                            pe.wait_ge(*act_ready(l, i - 1))
                        product(bank[bk][:, :], xgT[:, s, :], wide(p, 512), C).then_inc(gate_done.sem, 1)
                    if dn:
                        pe.wait_ge(*act_ready(l, i))
                        if a >= 2:
                            pe.wait_ge(*actT_lo(l, i - 1))
                        for q in range(FC):
                            ins = nc.tensor.transpose(bank[7][:, q * P:(q + 1) * P], act_[:, (a - 1) % 2, q::FC], ident[:, :])
                        ins.then_inc(act_tp.sem, 1)
                    if xt:
                        pe.wait_ge(*gathered[(a + 1) % 2](l, k + (a + 1) // 2 + 1))
                        if a >= 0:
                            pe.wait_ge(*xg_out(l, 2 * i + 2))
                        rows_half((a + 1) % 2, 0).then_inc(xg_tp.sem, 1)
                    if gu:
                        use(p + 1, k)
                        product(bank[bk + 1][:, :], xgT[:, s, :], wide(p + 1, 512), C).then_inc(gate_up.sem, 1)
                    if xt:
                        pe.wait_ge(*xg_out(l, 2 * i + 3))
                        rows_half((a + 1) % 2, 1).then_inc(xg_tp.sem, 1)
                    if dn:
                        if gu:
                            pe.wait_ge(*d_lo(l, 2 * i))
                            pe.wait_ge(*actT_lo(l, i))
                        else:
                            use(down_piece(l, a), k)
                            pe.wait_ge(*actT_out(l, i))
                        if a >= 2:
                            pe.wait_ge(*y_out(l, 2 * i - 2))
                        w = [v.rearrange("p (c n) -> p c n", c=FC) for v in down_r]
                        v = actT_r[:, (a - 1) % 2, :, :]
                        w32 = piece(down_piece(l, a)).rearrange("p (c n) -> p c n", c=FC)
                        for n in range(2):
                            cols = slice(512 * n, 512 * n + 512)
                            if not gu:
                                ins = product(bank[4 + n][:, :], actT[:, (a - 1) % 2, :], w32[:, :, cols], FC)
                            for c in range(FC if gu else 0):
                                rs = slice(c * P, (c + 1) * P)
                                mm(bank[4 + n][:, :], v[:, 0, rs], w[0][:, c, cols], c == 0, False)
                                mm(bank[4 + n][:, :], v[:, 0, rs], w[1][:, c, cols], False, False)
                                ins = mm(bank[4 + n][:, :], v[:, 1, rs], w[0][:, c, cols], False, c == FC - 1)
                            ins.then_inc(down.sem, 1)

                moe_step(0, -1, gu=False, dn=False)
                moe_step(0, 0, dn=False)
                moe_step(0, 1)
                moe_step(0, 2)
                with pe.Fori(0, 6) as k:
                    moe_step(k, 3)
                    moe_step(k, 4)
                moe_step(0, 15, xt=False)
                moe_step(0, 16, gu=False, xt=False)
                more = pe.value_load(over[0:1, 0:1], min_val=0, max_val=1)
                with pe.If(more > 0):
                    op = over_pe[l].sem
                    pe.wait_ge(*y_out(l, 2 * E))
                    pe.sem_inc(op, 1)
                    with pe.Fori(0, E) as e:
                        with pe.Fori(0, 3) as r:
                            n = 3 * e + r
                            pe.wait_ge(over_x[l].sem, 16 * n + 16)
                            rows_half(0, 0).then_inc(op, 1)
                            pe.wait_ge(over_dve[l].sem, 3 * n + 1)
                            rows_half(0, 1).then_inc(op, 1)
                            pe.wait_ge(over_dve[l].sem, 3 * n + 2)
                            pe.wait_ge(over_w[l].sem, 48 * n + 48)
                            product(bank[0][:, :], xgT[:, 0, :], ring[:, 0, :].rearrange("p (c n) -> p c n", c=C), C)
                            product(bank[1][:, :], xgT[:, 0, :], ring[:, 1, :].rearrange("p (c n) -> p c n", c=C), C).then_inc(op, 1)
                            pe.wait_ge(over_dve[l].sem, 3 * n + 3)
                            for q in range(FC):
                                ins = nc.tensor.transpose(bank[7][:, q * P:(q + 1) * P], act_[:, 0, q::FC], ident[:, :])
                            ins.then_inc(op, 1)
                            pe.wait_ge(over_act[l].sem, 4 * n + 2)
                            w = ring[:, 2, :].rearrange("p (c n) -> p c n", c=FC)
                            for q in range(2):
                                ins = product(bank[4 + q][:, :], actT[:, 0, :], w[:, :, 512 * q:512 * q + 512], FC)
                            ins.then_inc(op, 1)
                            pe.wait_ge(over_y[l].sem, 16 * n + 16)
                pe.end_ifs()


NAMES = ["x", "mem", "positions", "norm_mix", "w_in", "lam_q1", "lam_k1", "lam_q2", "lam_k2", "subln_a",
         "norm_b_out", "sgu_norm", "w_spatial", "b_spatial", "norm_c_out", "w_out", "norm_cross", "norm_mem",
         "w_cq", "w_ck", "w_cv", "w_co", "norm_ffn", "w_group", "b_group", "w_router", "b_router",
         "w_gate", "w_up", "w_down", "norm_final"]


def kernel(**inputs):
    import concourse.bacc as bacc
    from concourse.bass_utils import run_bass_kernel_spmd

    nc = bacc.Bacc("TRN2", target_bir_lowering=False, num_devices=1)
    arrays, args = {}, []
    for name in NAMES:
        a = np.ascontiguousarray(inputs[name])
        arrays[f"in_{name}"] = a
        args.append(nc.dram_tensor(f"in_{name}", a.shape, mybir.dt.from_np(a.dtype), kind="ExternalInput").ap())
    args.append(nc.dram_tensor("out", (1, S, D), F32, kind="ExternalOutput").ap())
    trunk(nc, *args)
    return run_bass_kernel_spmd(nc, [arrays], core_ids=[0]).results[0]["out"]
```
